# Optimizing a Trainium2 kernel written in Bass

```python
import math
import jax, jax.numpy as jnp
from jax import lax
import numpy as np

D_MODEL = 2048
BATCH = 1
SEQ = 256
DEPTH = 1

N_MEM = 256
EPS = 1e-6

DA_HEADS = 8
DA_QK_DIM = 64
DA_V_DIM = 2 * DA_QK_DIM
DA_ROT_DIM = DA_QK_DIM // 4
ROPE_THETA = 500000.0
Q_BLOCK = 128

RET_HEADS = 8
RET_QK_DIM = 64
RET_V_DIM = 128
RET_ROT_BASE = 10000.0
RET_CHUNK = 128

MEM_HEADS = 4
MEM_HEAD_DIM = 256

D_FF = 256 * (-(-(8 * D_MODEL) // (3 * 256)))

DA_Q_W = DA_HEADS * 2 * DA_QK_DIM
DA_K_W = DA_HEADS * 2 * DA_QK_DIM
DA_V_W = DA_HEADS * DA_V_DIM
RET_Q_W = RET_HEADS * RET_QK_DIM
RET_K_W = RET_HEADS * RET_QK_DIM
RET_V_W = RET_HEADS * RET_V_DIM
RET_G_W = RET_HEADS * RET_V_DIM
MEM_W = MEM_HEADS * MEM_HEAD_DIM
N_BRANCH = 3
GATE_W = N_BRANCH * D_MODEL
IN_SIZES = (DA_Q_W, DA_K_W, DA_V_W, RET_Q_W, RET_K_W, RET_V_W, RET_G_W, MEM_W, GATE_W)
IN_COLS = DA_Q_W + DA_K_W + DA_V_W + RET_Q_W + RET_K_W + RET_V_W + RET_G_W + MEM_W + GATE_W

kernel_name = 'hybrid_diffattn_retention_memxattn_swiglu'

def _rms_norm(x, g):
    xf = x.astype(jnp.float32)
    out = xf * lax.rsqrt(jnp.mean(xf * xf, axis=-1, keepdims=True) + EPS)
    return (out * g.astype(jnp.float32)).astype(x.dtype)

def _rope(x, positions, rot_dim, theta):
    half = rot_dim // 2
    inv_freq = theta ** (-jnp.arange(half, dtype=jnp.float32) * 2.0 / rot_dim)
    ang = positions.astype(jnp.float32)[..., None] * inv_freq
    cos = jnp.cos(ang)[:, :, None, :]
    sin = jnp.sin(ang)[:, :, None, :]
    xf = x.astype(jnp.float32)
    x1 = xf[..., :half]
    x2 = xf[..., half:rot_dim]
    out = jnp.concatenate([x1 * cos - x2 * sin, x2 * cos + x1 * sin, xf[..., rot_dim:]], axis=-1)
    return out.astype(x.dtype)

def _split_cols(t, sizes):
    outs, start = [], 0
    for s in sizes:
        outs.append(t[..., start:start + s])
        start += s
    return outs

def _diff_attention(q, k, v, q_g, k_g, lq1, lk1, lq2, lk2, subln_g, positions, lambda_init):
    B, S, _ = q.shape
    H, d, dv = DA_HEADS, DA_QK_DIM, DA_V_DIM
    q = _rms_norm(q.reshape(B, S, H * 2, d), q_g)
    k = _rms_norm(k.reshape(B, S, H * 2, d), k_g)
    q = _rope(q, positions, DA_ROT_DIM, ROPE_THETA).astype(jnp.float32)
    k = _rope(k, positions, DA_ROT_DIM, ROPE_THETA).astype(jnp.float32)
    v = v.reshape(B, S, H, dv).astype(jnp.float32)
    lam = (jnp.exp(jnp.sum(lq1.astype(jnp.float32) * lk1.astype(jnp.float32)))
           - jnp.exp(jnp.sum(lq2.astype(jnp.float32) * lk2.astype(jnp.float32))) + lambda_init)
    scale = d ** -0.5
    nb = S // Q_BLOCK
    qb = q.reshape(B, nb, Q_BLOCK, H, 2, d).transpose(1, 0, 3, 4, 2, 5)
    kh = k.reshape(B, S, H, 2, d).transpose(0, 2, 3, 1, 4)
    vh = v.transpose(0, 2, 1, 3)
    key_pos = jnp.arange(S)

    def attend_block(args):
        q_blk, blk = args
        s = jnp.einsum('bhmqd,bhmkd->bhmqk', q_blk, kh) * scale
        q_pos = blk * Q_BLOCK + jnp.arange(Q_BLOCK)
        causal = key_pos[None, :] <= q_pos[:, None]
        s = jnp.where(causal, s, -jnp.inf)
        p = jax.nn.softmax(s, axis=-1)
        a = p[:, :, 0] - lam * p[:, :, 1]
        return jnp.einsum('bhqk,bhkv->bhqv', a, vh)

    o = lax.map(attend_block, (qb, jnp.arange(nb)))
    o = o.transpose(1, 0, 3, 2, 4).reshape(B, S, H, dv)
    o = _rms_norm(o, subln_g) * (1.0 - lambda_init)
    return o.reshape(B, S, H * dv)

def _retention(q, k, v, g, norm_g, positions):
    B, S, _ = q.shape
    H, dk, dv, C = RET_HEADS, RET_QK_DIM, RET_V_DIM, RET_CHUNK
    q = _rope(q.reshape(B, S, H, dk), positions, dk, RET_ROT_BASE).astype(jnp.float32)
    k = _rope(k.reshape(B, S, H, dk), positions, dk, RET_ROT_BASE).astype(jnp.float32) * (dk ** -0.5)
    v = v.reshape(B, S, H, dv).astype(jnp.float32)
    log_gamma = jnp.log(1.0 - 2.0 ** (-5.0 - jnp.arange(H, dtype=jnp.float32)))
    idx = jnp.arange(C, dtype=jnp.float32)
    rel = idx[:, None] - idx[None, :]
    inner_decay = jnp.where(rel >= 0, jnp.exp(log_gamma[:, None, None] * jnp.maximum(rel, 0.0)), 0.0)
    query_decay = jnp.exp(log_gamma[:, None] * (idx + 1.0))
    key_decay = jnp.exp(log_gamma[:, None] * (C - 1.0 - idx))
    chunk_decay = jnp.exp(log_gamma * C)
    nc = S // C

    def to_chunks(t):
        return t.reshape(B, nc, C, H, t.shape[-1]).transpose(1, 0, 3, 2, 4)

    def step(state, inp):
        qc, kc, vc = inp
        scores = jnp.einsum('bhnd,bhmd->bhnm', qc, kc) * inner_decay
        o_in = jnp.einsum('bhnm,bhmv->bhnv', scores, vc)
        o_cross = jnp.einsum('bhnd,bhdv->bhnv', qc, state) * query_decay[:, :, None]
        state = state * chunk_decay[:, None, None] + jnp.einsum('bhmd,bhmv->bhdv', kc * key_decay[:, :, None], vc)
        return state, o_in + o_cross

    state0 = jnp.zeros((B, H, dk, dv), jnp.float32)
    _, o = lax.scan(step, state0, (to_chunks(q), to_chunks(k), to_chunks(v)))
    o = o.transpose(1, 0, 3, 2, 4).reshape(B, S, H, dv)
    o = _rms_norm(o, norm_g).reshape(B, S, H * dv)
    return jax.nn.silu(g.astype(jnp.float32)) * o

def _memory_attention(q, mem, mem_norm_g, w_mem_kv, q_g, k_g):
    B, S, _ = q.shape
    M = mem.shape[1]
    H, d = MEM_HEADS, MEM_HEAD_DIM
    m = _rms_norm(mem, mem_norm_g)
    kv = m @ w_mem_kv
    k, v = kv[..., :MEM_W], kv[..., MEM_W:]
    q = _rms_norm(q.reshape(B, S, H, d), q_g).astype(jnp.float32)
    k = _rms_norm(k.reshape(B, M, H, d), k_g).astype(jnp.float32)
    v = v.reshape(B, M, H, d).astype(jnp.float32)
    s = jnp.einsum('bshd,bmhd->bhsm', q, k) * (d ** -0.5)
    p = jax.nn.softmax(s, axis=-1)
    o = jnp.einsum('bhsm,bmhd->bshd', p, v)
    return o.reshape(B, S, H * d)

def setup_inputs(seed: int = 0) -> dict:
    key = jax.random.key(seed)
    ks = jax.random.split(key, 32)
    f32 = jnp.float32

    def w(k, shape, fan_in):
        return jax.random.normal(k, shape, f32) * (fan_in ** -0.5)

    def gain(k, shape):
        return 1.0 + 0.02 * jax.random.normal(k, shape, f32)

    L, D = DEPTH, D_MODEL
    return {
        'x': jax.random.normal(ks[0], (BATCH, SEQ, D), f32),
        'mem': jax.random.normal(ks[1], (BATCH, N_MEM, D), f32),
        'positions': jnp.broadcast_to(jnp.arange(SEQ, dtype=jnp.int32)[None, :], (BATCH, SEQ)),
        'attn_norm_g': gain(ks[2], (L, D)),
        'w_in': w(ks[3], (L, D, IN_COLS), D),
        'da_q_norm_g': gain(ks[4], (L, DA_QK_DIM)),
        'da_k_norm_g': gain(ks[5], (L, DA_QK_DIM)),
        'da_lambda_q1': 0.1 * jax.random.normal(ks[6], (L, DA_QK_DIM), f32),
        'da_lambda_k1': 0.1 * jax.random.normal(ks[7], (L, DA_QK_DIM), f32),
        'da_lambda_q2': 0.1 * jax.random.normal(ks[8], (L, DA_QK_DIM), f32),
        'da_lambda_k2': 0.1 * jax.random.normal(ks[9], (L, DA_QK_DIM), f32),
        'da_subln_g': gain(ks[10], (L, DA_V_DIM)),
        'ret_norm_g': gain(ks[11], (L, RET_V_DIM)),
        'mem_norm_g': gain(ks[12], (L, D)),
        'w_mem_kv': w(ks[13], (L, D, 2 * MEM_W), D),
        'mem_q_norm_g': gain(ks[14], (L, MEM_HEAD_DIM)),
        'mem_k_norm_g': gain(ks[15], (L, MEM_HEAD_DIM)),
        'w_o_da': w(ks[16], (L, DA_V_W, D), DA_V_W),
        'w_o_ret': w(ks[17], (L, RET_V_W, D), RET_V_W),
        'w_o_mem': w(ks[18], (L, MEM_W, D), MEM_W),
        'w_out': w(ks[19], (L, D, D), D),
        'ffn_norm_g': gain(ks[20], (L, D)),
        'w_ffn_gate': w(ks[21], (L, D, D_FF), D),
        'w_ffn_up': w(ks[22], (L, D, D_FF), D),
        'w_ffn_down': w(ks[23], (L, D_FF, D), D_FF),
    }

def reference(x, mem, positions, attn_norm_g, w_in, da_q_norm_g, da_k_norm_g,
              da_lambda_q1, da_lambda_k1, da_lambda_q2, da_lambda_k2, da_subln_g,
              ret_norm_g, mem_norm_g, w_mem_kv, mem_q_norm_g, mem_k_norm_g,
              w_o_da, w_o_ret, w_o_mem, w_out, ffn_norm_g, w_ffn_gate, w_ffn_up, w_ffn_down):
    for l in range(DEPTH):
        lambda_init = 0.8 - 0.6 * math.exp(-0.3 * l)
        h = _rms_norm(x, attn_norm_g[l])
        proj = h @ w_in[l]
        da_q, da_k, da_v, r_q, r_k, r_v, r_g, m_q, gates = _split_cols(proj, IN_SIZES)
        o_da = _diff_attention(da_q, da_k, da_v, da_q_norm_g[l], da_k_norm_g[l],
                               da_lambda_q1[l], da_lambda_k1[l], da_lambda_q2[l], da_lambda_k2[l],
                               da_subln_g[l], positions, lambda_init).astype(x.dtype)
        o_ret = _retention(r_q, r_k, r_v, r_g, ret_norm_g[l], positions).astype(x.dtype)
        o_mem = _memory_attention(m_q, mem, mem_norm_g[l], w_mem_kv[l],
                                  mem_q_norm_g[l], mem_k_norm_g[l]).astype(x.dtype)
        g_da, g_ret, g_mem = _split_cols(gates, (D_MODEL, D_MODEL, D_MODEL))
        merged = (jax.nn.sigmoid(g_da) * (o_da @ w_o_da[l])
                  + jax.nn.sigmoid(g_ret) * (o_ret @ w_o_ret[l])
                  + jax.nn.sigmoid(g_mem) * (o_mem @ w_o_mem[l]))
        x = x + merged @ w_out[l]
        hf = _rms_norm(x, ffn_norm_g[l])
        x = x + (jax.nn.silu(hf @ w_ffn_gate[l]) * (hf @ w_ffn_up[l])) @ w_ffn_down[l]
    return x


_drawn_inputs = setup_inputs


def setup_inputs(seed=0):
    import zlib

    import numpy as np

    out = dict(_drawn_inputs(seed))
    spreads = {}
    factors = {'attn_norm_g': 2.802,
     'da_q_norm_g': 7.353,
     'da_k_norm_g': 6.263,
     'da_lambda_q1': 5.128,
     'da_lambda_k2': 8.0,
     'da_subln_g': 5.853,
     'ret_norm_g': 8.0,
     'mem_norm_g': 8.0,
     'mem_q_norm_g': 8.0,
     'mem_k_norm_g': 8.0,
     'ffn_norm_g': 4.287}
    for name, (base, spread) in spreads.items():
        noise = np.random.default_rng([zlib.crc32(name.encode()), seed]).standard_normal(out[name].shape)
        drawn = base * np.exp(spread * noise) if base else spread * noise
        out[name] = __import__('jax').numpy.asarray(drawn.astype(out[name].dtype))
    for name, factor in factors.items():
        out[name] = (out[name] * factor).astype(out[name].dtype)
    return out
```

```python
from contextlib import ExitStack

import numpy as np

import concourse.bass as bass
from concourse import mybir

F32 = mybir.dt.float32
F32R = mybir.dt.float32r
I32 = mybir.dt.int32
ALU = mybir.AluOpType
ACT = mybir.ActivationFunctionType
AX = mybir.AxisListType

P = 128
D = 2048
TB = 2
TOK = TB * P
NCOL = 512
KD = D // P
EPS = 1e-6
LAMBDA_INIT = 0.2

DA_H, DA_D, DA_V, DA_ROT = 8, 64, 128, 16
RT_H, RT_D, RT_V = 8, 64, 128
MEM_H, MEM_D = 4, 256
DA_THETA, RT_THETA = 500000.0, 10000.0
D_FF = 5632
NF = D_FF // NCOL

DA_Q0, DA_K0, DA_V0 = 0, 1024, 2048
RT_Q0, RT_K0, RT_V0, RT_G0 = 3072, 3584, 4096, 5120
MQ0, GATE0 = 6144, 7168
GATE_DA, GATE_RT, GATE_MEM = GATE0, GATE0 + D, GATE0 + 2 * D

RING = 4
G_KV, G_MQ, G_PROJ, G_MB, G_DB, G_RB, G_OUT, G_F0, G_F = 0, 32, 48, 144, 192, 240, 288, 320, 336
G_END = G_F + 24 * (NF - 1)
PAIRS = G_END + 8
U_KV, U_MQ, U_PROJ, U_MB, U_DB, U_RB, U_OUT, U_F0, U_F = 0, 2, 3, 9, 13, 17, 21, 23, 24
U_END = U_F + 3 * (NF - 1)
NEG = -1.0e30
FAR = 3.0e7
TWO_PI = (6.28125, 0.0019350051879882812, 3.019916050173085e-07)
ROUND = 12582912.0


def shape_constants():
    da = np.float32(DA_THETA) ** (-np.arange(DA_ROT // 2, dtype=np.float32) * np.float32(2.0) / np.float32(DA_ROT))
    rt = np.float32(RT_THETA) ** (-np.arange(RT_D // 2, dtype=np.float32) * np.float32(2.0) / np.float32(RT_D))
    lg = np.log(np.float32(1.0) - np.float32(2.0) ** (np.float32(-5.0) - np.arange(RT_H, dtype=np.float32)))
    return np.concatenate([da, rt, lg]).astype(np.float32)[None, :]


def program(nc, x, mem, positions, attn_norm_g, w_in, da_q_norm_g, da_k_norm_g, da_lambda_q1, da_lambda_k1,
            da_lambda_q2, da_lambda_k2, da_subln_g, ret_norm_g, mem_norm_g, w_mem_kv, mem_q_norm_g,
            mem_k_norm_g, w_o_da, w_o_ret, w_o_mem, w_out, ffn_norm_g, w_ffn_gate, w_ffn_up, w_ffn_down,
            shape_consts, out):
    ds = bass.ds
    NROT = DA_ROT // 2 + RT_D // 2
    R1 = DA_ROT // 2
    with ExitStack() as ctx:
        def sb(name, shape, dt=F32):
            return ctx.enter_context(nc.sbuf_tensor(name, shape, dt))

        def sem(name):
            return ctx.enter_context(nc.semaphore(name))

        raw = sb("raw", [P, RING, 2, NCOL])
        w_hi = sb("w_hi", [P, RING, 2, NCOL], F32R)
        w_lo = sb("w_lo", [P, RING, 2, NCOL], F32R)
        hT_hi = sb("hT_hi", [P, KD, TOK], F32R)
        hT_lo = sb("hT_lo", [P, KD, TOK], F32R)
        oT_hi = sb("oT_hi", [P, KD, TOK], F32R)
        oT_lo = sb("oT_lo", [P, KD, TOK], F32R)
        proj = sb("proj", [P, TB, GATE0])
        kvm = sb("kvm", [P, TB, D])
        sq = sb("sq", [P, TB, 2, 256])
        qn = sb("qn", [P, TB, 2, 256])
        pm = sb("pm", [P, 4, 384])
        ident = sb("ident", [P, P])
        mask = sb("mask", [P, P])
        rel = sb("rel", [P, 256])
        g_cols = sb("g_cols", [P, 3 * KD])
        g_da = sb("g_da", [P, 2, DA_D])
        g_mem = sb("g_mem", [P, 2, MEM_D])
        g_sub = sb("g_sub", [P, DA_V])
        g_ret = sb("g_ret", [P, RT_V])
        lam_s = sb("lam_s", [P, 2])
        lam_e = sb("lam_e", [P, 2])
        neg_lam = sb("neg_lam", [P, 1])
        sc = sb("sc", [P, NROT + RT_H])
        pos_i = sb("pos_i", [P, TB], I32)
        pos_f = sb("pos_f", [P, TB])
        trig = sb("trig", [P, 2, TB, NROT])
        minus_half = sb("minus_half", [P, 16])
        ss = sb("ss", [P, 16])
        ms = sb("ms", [P, 16])
        rstd = sb("rstd", [P, 16])
        row_ss = sb("row_ss", [P, 3, TB])
        row_ms = sb("row_ms", [P, 3, TB])
        row_rstd = sb("row_rstd", [P, 3, TB])
        mx = sb("mx", [P, 4, 2])
        nmx = sb("nmx", [P, 4, 2])
        den = sb("den", [P, 4, 2])
        rden = sb("rden", [P, 4, 2])
        lrden = sb("lrden", [P, 2, 2])

        sq_flat, qn_flat, pm_flat = (a[:].rearrange(r) for a, r in (
            (sq, "p t k d -> p (t k d)"), (qn, "p t k d -> p (t k d)"), (pm, "p b c -> p (b c)")))
        qkT = sq_flat.rearrange("p (j c) -> p j c", j=2)
        pT = qn_flat[:, 0:768].rearrange("p (j c) -> p j c", j=2)
        osb = pm_flat[:, 0:512].rearrange("p (a c) -> p a c", a=2)
        tmp = pm_flat[:, 0:512].rearrange("p (n c) -> p n c", n=4)
        dec = pm_flat[:, 768:1280].rearrange("p (j c) -> p j c", j=2)
        tanh_g = qn[:, :, :, P:2 * P]
        lam_in = pm_flat[:, 0:256].rearrange("p (a b d) -> p a b d", a=2, b=2)
        lam_pr = pm_flat[:, 256:384].rearrange("p (b d) -> p b d", b=2)
        ang = pm_flat[:, 384:544].rearrange("p (k t n) -> p k t n", k=2, t=TB)
        turns = pm_flat[:, 544:704].rearrange("p (k t n) -> p k t n", k=2, t=TB)
        g_rows = pm_flat[0:3 * KD, 768:768 + P]
        gt = proj[:, :, MQ0:MQ0 + NCOL]
        sg = proj[:, :, MQ0 + NCOL:MQ0 + 2 * NCOL]

        acc = [ctx.enter_context(nc.psum_tensor(f"acc{i}", [P, TB, NCOL], F32)) for i in range(2)]
        at = ctx.enter_context(nc.psum_tensor("at", [P, 4, 512], F32))

        loaded = [sem(f"loaded{i}") for i in range(RING)]
        hi_done, lo_done, pair_used = sem("hi_done"), sem("lo_done"), sem("pair_used")
        acc_ready = [sem(f"acc_ready{i}") for i in range(2)]
        acc_free = [sem(f"acc_free{i}") for i in range(2)]
        mem_in, x_in = [sem(f"mem_in{i}") for i in range(2)], [sem(f"x_in{i}") for i in range(2)]
        x_again = sem("x_again")
        const_in = sem("const_in")
        zeroed, masks = sem("zeroed"), sem("masks")
        gcol_ps, gcol_ok = sem("gcol_ps"), sem("gcol_ok")
        row_sq, row_mean, row_root = sem("row_sq"), sem("row_mean"), sem("row_root")
        row_ok = sem("row_ok")
        col_ps, col_hi, col_lo = sem("col_ps"), sem("col_hi"), sem("col_lo")
        setup_v, setup_a = sem("setup_v"), sem("setup_a")
        out_done = sem("out_done")

        def phase_sems(tag, names):
            return {n: sem(f"{tag}_{n}") for n in names}
        M = phase_sems("mem", "squared summed mean root normed turned copied scored maxed negmax exped recip "
                              "pT_ps pT ov onorm oT_ps hi lo".split())
        A = phase_sems("da", "squared summed mean root scaled gained rprod rot turned copied scored masked maxed negmax "
                             "exped recip lrecip second mixed pT_ps pT ov osq osum omean oroot onorm oT_ps hi lo".split())
        R = phase_sems("ret", "decays tanh rprod rot turned copied scored weighed ov osq osum omean oroot onorm gmul "
                              "gated oT_ps hi lo".split())
        branch_out, merged = sem("branch_out"), sem("merged")
        x2_done = sem("x2_done")
        ff_gate, ff_act, ff_ps, ff_hi, ff_lo = sem("ff_gate"), sem("ff_act"), sem("ff_ps"), sem("ff_hi"), sem("ff_lo")

        block = ctx.enter_context(nc.Block())

        def tiles(w, row0, col0):
            return w[ds(row0, 2 * P), ds(col0, NCOL)].rearrange("(k p) n -> p k n", p=P)

        w_in2, w_kv2, w_out2 = w_in[0], w_mem_kv[0], w_out[0]
        w_g2, w_u2, w_d2 = w_ffn_gate[0], w_ffn_up[0], w_ffn_down[0]

        @block.sync
        def _(sp):
            def load(w, row0, col0, g, s):
                if not (isinstance(g, int) and g < RING):
                    sp.wait_ge(lo_done, g - RING + 1)
                sp.dma_start(raw[:, s % RING], tiles(w, row0, col0)).then_inc(loaded[s % RING], 16)

            def load_chunk(w, row0, col0, g, s, n=KD // 2):
                for k in range(n):
                    load(w, row0 + 2 * P * k, col0, g + k, s + k)

            for t in range(TB):
                sp.dma_start(proj[:, t, 0:D], mem[0, t * P:(t + 1) * P, :]).then_inc(mem_in[t], 16)
            for k in range(4):
                load(w_kv2, 2 * P * k, 0, k, k)
            for t in range(TB):
                sp.dma_start(proj[:, t, D:2 * D], x[0, t * P:(t + 1) * P, :]).then_inc(x_in[t], 16)
            for k in range(4, 8):
                load(w_kv2, 2 * P * k, 0, k, k)
            with sp.Fori(1, 4) as n:
                load_chunk(w_kv2, 0, n * NCOL, G_KV + n * 8, 0)
            with sp.Fori(0, 2) as n:
                load_chunk(w_in2, 0, n * NCOL + MQ0, n * 8 + G_MQ, 0)
            with sp.Fori(0, 12) as n:
                load_chunk(w_in2, 0, n * NCOL, n * 8 + G_PROJ, 0)
            for gate, wo, g0 in ((GATE_MEM, w_o_mem, G_MB), (GATE_DA, w_o_da, G_DB), (GATE_RT, w_o_ret, G_RB)):
                with sp.Fori(1, 5) as n:
                    load_chunk(w_in2, 0, n * NCOL + (gate - NCOL), n * 12 + (g0 - 12), 0)
                    load_chunk(wo[0], 0, n * NCOL - NCOL, n * 12 + (g0 - 4), 8, 4)
                if gate == GATE_DA:
                    sp.wait_ge(A["lo"], 4)
                    for t in range(TB):
                        sp.dma_start(proj[:, t, 0:D], x[0, t * P:(t + 1) * P, :]).then_inc(x_again, 16)
            with sp.Fori(0, 4) as n:
                load_chunk(w_out2, 0, n * NCOL, n * 8 + G_OUT, 0)
            load_chunk(w_g2, 0, 0, G_F0, 0)
            load_chunk(w_u2, 0, 0, G_F0 + 8, 8)
            with sp.Fori(1, NF) as f:
                g0 = f * 24 + (G_F - 24)
                load_chunk(w_g2, 0, f * NCOL, g0, 0)
                load_chunk(w_u2, 0, f * NCOL, g0 + 8, 8)
                for n in range(4):
                    load_chunk(w_d2, f * NCOL - NCOL, n * NCOL, g0 + (16 + 2 * n), 2 * n, 2)
            for n in range(4):
                load_chunk(w_d2, (NF - 1) * NCOL, n * NCOL, G_END + 2 * n, 2 * n, 2)
            for n in range(4):
                sp.wait_ge(x2_done, 4 * NF + n + 1)
                sp.dma_start(out[0].rearrange("(t p) n -> p t n", p=P)[:, :, n * NCOL:(n + 1) * NCOL],
                             proj[:, :, n * NCOL:(n + 1) * NCOL]).then_inc(out_done, 16)
            sp.wait_ge(out_done, 64)

        @block.gpsimd
        def _(pool):
            nc.gpsimd.memset(ident[:], 0.0).then_inc(zeroed, 1)
            nc.gpsimd.memset(mask[:], 0.0).then_inc(zeroed, 1)
            nc.gpsimd.memset(minus_half[:], -0.5).then_inc(zeroed, 1)
            nc.gpsimd.iota(rel[:], pattern=[[1, 256]], base=0, channel_multiplier=-1,
                           allow_small_or_imprecise_dtypes=True).then_inc(zeroed, 1)
            pool.wait_ge(zeroed, 4)
            nc.gpsimd.affine_select(out=ident[:], in_=ident[:], compare_op=ALU.not_equal, fill=1.0, base=0,
                                    pattern=[[-1, P]], channel_multiplier=1).then_inc(masks, 1)
            nc.gpsimd.affine_select(out=mask[:], in_=mask[:], compare_op=ALU.is_ge, fill=NEG, base=0,
                                    pattern=[[-1, P]], channel_multiplier=1).then_inc(masks, 1)
            nc.gpsimd.affine_select(out=rel[:], in_=rel[:], compare_op=ALU.is_ge, fill=FAR, base=0,
                                    pattern=[[1, 256]], channel_multiplier=-1).then_inc(masks, 1)

            def row_roots(k):
                for t in range(TB):
                    pool.wait_ge(row_mean, 2 * k + t + 1)
                    nc.gpsimd.tensor_tensor(row_rstd[:, k, t:t + 1], row_ms[:, k, t:t + 1], minus_half[:, 0:1],
                                            ALU.pow).then_inc(row_root, 1)

            def head_roots(ready, done, i, n):
                pool.wait_ge(ready, i + 1)
                nc.gpsimd.tensor_tensor(rstd[:, 0:n], ms[:, 0:n], minus_half[:, 0:n], ALU.pow).then_inc(done, 1)

            row_roots(0)
            row_roots(1)
            with pool.Fori(0, MEM_H) as i:
                head_roots(M["mean"], M["root"], i, 4)
            with pool.Fori(0, 4) as i:
                head_roots(A["mean"], A["root"], i, 16)
                head_roots(A["omean"], A["oroot"], i, 4)
            with pool.Fori(0, 4) as i:
                head_roots(R["omean"], R["oroot"], i, 4)
            row_roots(2)

        @block.scalar
        def _(act):
            def const(dst, src):
                act.dma_start(dst, src).then_inc(const_in, 16)

            for k, g in enumerate((mem_norm_g, attn_norm_g, ffn_norm_g)):
                const(g_rows[k * KD:(k + 1) * KD, :], g[0].rearrange("(k p) -> k p", p=P))
            for k, g in enumerate((da_q_norm_g, da_k_norm_g)):
                const(g_da[:, k, :], g[0].partition_broadcast(P))
            for k, g in enumerate((mem_q_norm_g, mem_k_norm_g)):
                const(g_mem[:, k, :], g[0].partition_broadcast(P))
            const(g_sub[:], da_subln_g[0].partition_broadcast(P))
            const(g_ret[:], ret_norm_g[0].partition_broadcast(P))
            for k, g in enumerate((da_lambda_q1, da_lambda_q2)):
                const(lam_in[:, 0, k, :], g[0].partition_broadcast(P))
            for k, g in enumerate((da_lambda_k1, da_lambda_k2)):
                const(lam_in[:, 1, k, :], g[0].partition_broadcast(P))
            const(sc[:], shape_consts[0].partition_broadcast(P))
            with nc.allow_non_contiguous_dma(reason="256 positions, once"):
                const(pos_i[:], positions[0].rearrange("(t p) -> p t", p=P))

            def high(g, s):
                act.wait_ge(loaded[s % RING], (g // RING + 2) * 16 if isinstance(g, int) else g * 4 + (32 - 4 * (s % RING)))
                act.wait_ge(pair_used, g + 1)
                act.activation(w_hi[:, s % RING], raw[:, s % RING], ACT.Copy).then_inc(hi_done, 1)

            def row_squares(k, ready, src, col0):
                for t in range(TB):
                    act.wait_ge(*ready(t))
                    act.activation(kvm[:, t, :], src[:, t, col0:col0 + D], ACT.Square,
                                   accum_out=row_ss[:, k, t:t + 1]).then_inc(row_sq, 1)

            def high_columns(n0, dst, scale):
                for k in range(KD):
                    act.wait_ge(col_ps, n0 + k + 1)
                    act.activation(dst[:, k, :], at[:, k % 4, 0:TOK], ACT.Copy, scale=scale(k)).then_inc(col_hi, 1)

            def evacuate(u, p, dst):
                act.wait_ge(acc_ready[p], u + 1)
                act.activation(dst, acc[p][:], ACT.Copy).then_inc(acc_free[p], 1)

            row_squares(0, lambda t: (mem_in[t], 16), proj, 0)
            for s in range(RING):
                act.wait_ge(loaded[s], 16)
                act.activation(w_hi[:, s], raw[:, s], ACT.Copy).then_inc(hi_done, 1)
            act.wait_ge(gcol_ok, 1)
            high_columns(0, oT_hi, lambda k: g_cols[:, k:k + 1])
            act.wait_ge(row_sq, 2)
            row_squares(1, lambda t: (x_in[t], 16), proj, D)

            with act.Fori(0, 2) as i:
                for s in range(16):
                    if s == 0:
                        act.wait_ge(row_sq, 4)
                    if s == 7:
                        evacuate(i + U_KV, 0, kvm[:, :, ds(i * 1024, 512)])
                    if s == 15:
                        evacuate(i + U_KV, 1, kvm[:, :, ds(i * 1024 + 512, 512)])
                    high(i * 16 + (G_KV + s), s)

            high_columns(KD, hT_hi, lambda k: g_cols[:, KD + k:KD + k + 1])
            act.wait_ge(setup_v, 11)
            act.activation(trig[:], ang, ACT.Sin).then_inc(setup_a, 1)
            act.activation(lam_e[:], lam_s[:], ACT.Exp).then_inc(setup_a, 1)
            for s in range(16):
                if s in (7, 15):
                    c0 = MQ0 + (s // 8) * NCOL
                    evacuate(U_MQ, s // 8, proj[:, :, c0:c0 + NCOL])
                high(G_MQ + s, s)

            def projections(i, s, i0):
                if s in (7, 15):
                    evacuate(i + (U_PROJ + i0), s // 8, proj[:, :, ds(i * 1024 + (1024 * i0 + (s // 8) * NCOL), NCOL)])
                high(i * 16 + (G_PROJ + 16 * i0 + s), s)

            with act.Fori(0, MEM_H) as i:
                for s in range(16):
                    if s == 0:
                        act.activation(sq[:, :, 0, :], proj[:, :, ds(i * MEM_D + MQ0, MEM_D)], ACT.Square)
                        act.activation(sq[:, :, 1, :], kvm[:, :, ds(i * MEM_D, MEM_D)],
                                       ACT.Square).then_inc(M["squared"], 1)
                    if s == 3:
                        act.wait_ge(M["turned"], i + 1)
                        act.activation(qkT, at[:, 0:2, :], ACT.Copy).then_inc(M["copied"], 1)
                    if s == 5:
                        act.wait_ge(M["negmax"], i + 1)
                        for t in range(TB):
                            e = act.activation(pm[:, t, 0:256], at[:, 2, t * 256:(t + 1) * 256], ACT.Exp,
                                               bias=nmx[:, 0, t:t + 1], scale=MEM_D ** -0.5,
                                               accum_out=den[:, 0, t:t + 1])
                        e.then_inc(M["exped"], 1)
                    if s == 7:
                        act.wait_ge(M["pT_ps"], i + 1)
                        act.activation(pT[:, :, 0:256], at[:, 3, :].rearrange("p (a b) -> p a b", a=2),
                                       ACT.Copy).then_inc(M["pT"], 1)
                    if s == 11:
                        act.wait_ge(M["oT_ps"], i + 1)
                        act.activation(oT_hi[:, ds(i * 2, 2), :], at[:, 1, :].rearrange("p (a b) -> p a b", a=2),
                                       ACT.Copy).then_inc(M["hi"], 1)
                    projections(i, s, 0)
            with act.Fori(0, 2) as i:
                for s in range(16):
                    projections(i, s, 4)

            def gate(i, s, u0):
                if s == 8:
                    act.wait_ge(acc_ready[0], i + (u0 + 1))
                    act.wait_ge(acc_free[1], i + (u0 + 1))
                    act.activation(sg, acc[0][:], ACT.Tanh, scale=0.5).then_inc(acc_free[0], 1)

            with act.Fori(0, 4) as i:
                for s in range(12):
                    if s == 0:
                        act.activation(sq[:, :, 0, :], proj[:, :, ds(i * 256 + DA_Q0, 256)], ACT.Square)
                        act.activation(sq[:, :, 1, :], proj[:, :, ds(i * 256 + DA_K0, 256)],
                                       ACT.Square).then_inc(A["squared"], 1)
                    if s == 3:
                        act.wait_ge(A["turned"], i + 1)
                        for j in range(2):
                            e = act.activation(qkT[:, j, :], at[:, 2 * j, :], ACT.Copy)
                        e.then_inc(A["copied"], 1)
                    if s == 6:
                        act.wait_ge(A["negmax"], i + 1)
                        for b in range(4):
                            for t, (c0, c1) in enumerate(((0, 128), (128, 384))):
                                e = act.activation(pm[:, b, c0:c1], at[:, b, c0:c1], ACT.Exp,
                                                   bias=nmx[:, b, t:t + 1], scale=DA_D ** -0.5,
                                                   accum_out=den[:, b, t:t + 1])
                        e.then_inc(A["exped"], 1)
                    gate(i, s, U_MB)
                    if s == 9:
                        act.wait_ge(A["pT_ps"], i + 1)
                        for j in range(2):
                            e = act.activation(pT[:, j, :], at[:, 2 * j, 0:384], ACT.Copy)
                        e.then_inc(A["pT"], 1)
                    if s == 10:
                        act.wait_ge(A["ov"], i + 1)
                        for j in range(2):
                            e = act.activation(sq[:, j, 0, :], at[:, 2 * j + 1, 0:256], ACT.Square)
                        e.then_inc(A["osq"], 1)
                    if s == 11:
                        act.wait_ge(A["oT_ps"], i + 1)
                        act.activation(oT_hi[:, ds(i * 2 + 8, 2), :], at[:, 0, :].rearrange("p (a b) -> p a b", a=2),
                                       ACT.Copy).then_inc(A["hi"], 1)
                    high(i * 12 + (G_MB + s), s)

            with act.Fori(0, 4) as i:
                for s in range(12):
                    if s == 0:
                        for j in range(2):
                            e = act.activation(dec[:, j, 0:256], rel[:], ACT.Exp, scale=sc[:, ds(i * 2 + (NROT + j), 1)])
                        e.then_inc(R["decays"], 1)
                        act.activation(tanh_g, proj[:, :, ds(i * 256 + RT_G0, 256)].rearrange(
                                           "p t (j d) -> p t j d", j=2), ACT.Tanh,
                                       scale=0.5).then_inc(R["tanh"], 1)
                    if s == 3:
                        act.wait_ge(R["turned"], i + 1)
                        act.activation(qkT[:, 0, :], at[:, 0, :], ACT.Copy).then_inc(R["copied"], 1)
                    if s == 7:
                        act.wait_ge(R["ov"], i + 1)
                        act.activation(sq[:, :, 0, :], at[:, 3, :].rearrange("p (a b) -> p a b", a=2),
                                       ACT.Square).then_inc(R["osq"], 1)
                    gate(i, s, U_DB)
                    if s == 10:
                        act.wait_ge(R["oT_ps"], i + 1)
                        act.activation(oT_hi[:, ds(i * 2, 2), :], at[:, 0, :].rearrange("p (a b) -> p a b", a=2),
                                       ACT.Copy).then_inc(R["hi"], 1)
                    high(i * 12 + (G_DB + s), s)

            with act.Fori(0, 4) as i:
                for s in range(12):
                    gate(i, s, U_RB)
                    high(i * 12 + (G_RB + s), s)

            high_columns(2 * KD, oT_hi, lambda k: 0.5)
            with act.Fori(0, 2) as i:
                for s in range(16):
                    high(i * 16 + (G_OUT + s), s)
            row_squares(2, lambda t: (x2_done, 4), proj, 0)
            high_columns(3 * KD, hT_hi, lambda k: g_cols[:, 2 * KD + k:2 * KD + k + 1])

            def silu(u, f):
                act.wait_ge(acc_ready[0], u + 1)
                if not isinstance(f, int):
                    act.wait_ge(ff_act, f)
                act.activation(sg, acc[0][:], ACT.Silu).then_inc(acc_free[0], 1)

            def high_acts(f):
                act.wait_ge(ff_ps, f)
                act.activation(oT_hi[:, 0:4, :], at[:, 0:2, :].rearrange("p b (a c) -> p (b a) c", a=2),
                               ACT.Copy).then_inc(ff_hi, 1)

            for s in range(16):
                if s == 8:
                    silu(U_F0, 0)
                high(G_F0 + s, s)
            with act.Fori(1, NF) as f:
                for s in range(24):
                    if s == 3:
                        high_acts(f)
                    if s == 8:
                        silu(f * 3 + (U_F - 3), f)
                    high(f * 24 + (G_F - 24 + s), s)
            high_acts(NF)
            for s in range(4):
                high(G_END + s, s)

        @block.vector
        def _(v):
            def step(ins, s, value):
                ins.then_inc(s, 1)
                v.wait_ge(s, value)

            def low(g, s):
                v.wait_ge(hi_done, g + (RING + 1))
                v.tensor_tensor(w_lo[:, s % RING], raw[:, s % RING], w_hi[:, s % RING].bitcast(F32),
                                ALU.subtract).then_inc(lo_done, 1)

            def scale_rows(k, src, dst, c0, c1):
                for t in range(TB):
                    v.wait_ge(row_sq, 2 * k + t + 1)
                    v.tensor_scalar(row_ms[:, k, t:t + 1], row_ss[:, k, t:t + 1], 1.0 / D, EPS, ALU.mult,
                                    ALU.add).then_inc(row_mean, 1)
                for t in range(TB):
                    v.wait_ge(row_root, 2 * k + t + 1)
                    v.tensor_scalar(dst[:, t, c1:c1 + D], src[:, t, c0:c0 + D], row_rstd[:, k, t:t + 1], None,
                                    ALU.mult).then_inc(row_ok, 1)

            def low_columns(n0, dst, hi, scale):
                for k in range(KD):
                    v.wait_ge(col_hi, n0 + k + 1)
                    v.scalar_tensor_tensor(out=dst[:, k, :], in0=at[:, k % 4, 0:TOK], scalar=scale(k),
                                           in1=hi[:, k, :].bitcast(F32), op0=ALU.mult,
                                           op1=ALU.subtract).then_inc(col_lo, 1)

            def mean_squares(src, n, width, i, X, summed, mean):
                step(v.tensor_reduce(ss[:, 0:n], src, AX.X, ALU.add), X[summed], i + 1)
                v.tensor_scalar(ms[:, 0:n], ss[:, 0:n], 1.0 / width, EPS, ALU.mult, ALU.add).then_inc(X[mean], 1)

            for p in range(2):
                v.nop().then_inc(acc_free[p], 1)
            scale_rows(0, proj, proj, 0, 0)
            for s in range(RING):
                v.wait_ge(hi_done, s + 1)
                v.tensor_tensor(w_lo[:, s], raw[:, s], w_hi[:, s].bitcast(F32), ALU.subtract).then_inc(lo_done, 1)
            v.wait_ge(gcol_ps, 1)
            step(v.tensor_copy(g_cols[:], at[:, 3, 0:3 * KD]), gcol_ok, 1)
            low_columns(0, oT_lo, oT_hi, lambda k: g_cols[:, k:k + 1])
            scale_rows(1, proj, proj, D, D)

            with v.Fori(0, 2) as i:
                for s in range(16):
                    low(i * 16 + (G_KV + s), s)

            v.wait_ge(const_in, 16 * 15)
            step(v.tensor_copy(pos_f[:], pos_i[:]), setup_v, 1)
            for t in range(TB):
                for k in range(2):
                    e = v.tensor_scalar(ang[:, k, t, :], sc[:, 0:NROT], pos_f[:, t:t + 1], None, ALU.mult)
            step(e, setup_v, 2)
            for k in range(2):
                e = v.tensor_scalar(turns[:, k], ang[:, k], 1.0 / (2.0 * np.pi), 0.25 * k, ALU.mult, ALU.add)
            step(e, setup_v, 3)
            step(v.tensor_scalar(turns, turns, ROUND, None, ALU.add), setup_v, 4)
            step(v.tensor_scalar(turns, turns, -ROUND, None, ALU.add), setup_v, 5)
            for n, part in enumerate(TWO_PI):
                step(v.scalar_tensor_tensor(out=ang, in0=turns, scalar=-part, in1=ang, op0=ALU.mult,
                                            op1=ALU.add), setup_v, 6 + n)
            v.tensor_tensor(lam_pr, lam_in[:, 0], lam_in[:, 1], ALU.mult)
            step(v.tensor_scalar(ang[:, 1], ang[:, 1], 0.5 * np.pi, None, ALU.add), setup_v, 9)
            step(v.tensor_scalar(ang, ang, 3.1415925, -3.1415925, ALU.min, ALU.max), setup_v, 10)
            v.tensor_reduce(lam_s[:], lam_pr[:], AX.X, ALU.add).then_inc(setup_v, 1)
            low_columns(KD, hT_lo, hT_hi, lambda k: g_cols[:, KD + k:KD + k + 1])
            v.wait_ge(setup_a, 2)
            step(v.tensor_tensor(neg_lam[:], lam_e[:, 1:2], lam_e[:, 0:1], ALU.subtract), setup_v, 12)
            v.tensor_scalar(neg_lam[:], neg_lam[:], -LAMBDA_INIT, None, ALU.add)
            v.tensor_scalar(g_sub[:], g_sub[:], 1.0 - LAMBDA_INIT, None, ALU.mult)
            step(v.tensor_scalar(g_ret[:], g_ret[:], 0.5, None, ALU.mult), setup_v, 13)

            for s in range(16):
                low(G_MQ + s, s)

            with v.Fori(0, MEM_H) as i:
                for s in range(16):
                    if s == 0:
                        v.wait_ge(M["squared"], i + 1)
                        mean_squares(sq[:].rearrange("p t k d -> p (t k) d"), 4, MEM_D, i, M, "summed", "mean")
                        v.wait_ge(M["root"], i + 1)
                        for t in range(TB):
                            for k, src in enumerate((proj[:, t, ds(i * MEM_D + MQ0, MEM_D)],
                                                     kvm[:, t, ds(i * MEM_D, MEM_D)])):
                                e = v.scalar_tensor_tensor(out=qn[:, t, k, :], in0=src,
                                                           scalar=rstd[:, 2 * t + k:2 * t + k + 1],
                                                           in1=g_mem[:, k, :], op0=ALU.mult, op1=ALU.mult)
                        e.then_inc(M["normed"], 1)
                    if s == 5:
                        v.wait_ge(M["scored"], i + 1)
                        step(v.tensor_reduce(mx[:, 0, :], at[:, 2, :].rearrange("p (t k) -> p t k", t=2), AX.X,
                                             ALU.max), M["maxed"], i + 1)
                        v.tensor_scalar(nmx[:, 0, :], mx[:, 0, :], -MEM_D ** -0.5, None,
                                        ALU.mult).then_inc(M["negmax"], 1)
                    if s == 6:
                        v.wait_ge(M["exped"], i + 1)
                        step(v.reciprocal(rden[:, 0, :], den[:, 0, :]), M["recip"], i + 1)
                    if s == 9:
                        v.wait_ge(M["ov"], i + 1)
                        for t in range(TB):
                            e = v.tensor_scalar(osb[:, t, :], at[:, 0, t * 256:(t + 1) * 256], rden[:, 0, t:t + 1],
                                                None, ALU.mult)
                        e.then_inc(M["onorm"], 1)
                    if s == 11:
                        v.wait_ge(M["hi"], i + 1)
                        v.tensor_tensor(oT_lo[:, ds(i * 2, 2), :], at[:, 1, :].rearrange("p (a b) -> p a b", a=2),
                                        oT_hi[:, ds(i * 2, 2), :].bitcast(F32), ALU.subtract).then_inc(M["lo"], 1)
                    low(i * 16 + (G_PROJ + s), s)
            with v.Fori(0, 2) as i:
                for s in range(16):
                    low(i * 16 + (G_PROJ + 64 + s), s)

            def gated(i, s, u0, first, n0):
                if s == 11:
                    v.wait_ge(acc_ready[1], i + (u0 + 1))
                    v.wait_ge(acc_free[0], i + (u0 + 2))
                    dst = kvm[:, :, ds(i * NCOL, NCOL)]
                    e = v.scalar_tensor_tensor(out=dst if first else gt, in0=sg, scalar=1.0, in1=acc[1][:],
                                               op0=ALU.add, op1=ALU.mult)
                    e.then_inc(acc_free[1], 1)
                    if not first:
                        v.wait_ge(acc_free[1], i + (u0 + 2))
                        v.tensor_tensor(dst, dst, gt, ALU.add).then_inc(merged, 1)
                        v.wait_ge(merged, i + (n0 + 1))

            with v.Fori(0, 4) as i:
                for s in range(12):
                    if s == 0:
                        v.wait_ge(A["squared"], i + 1)
                        mean_squares(sq[:].rearrange("p t k (m d) -> p (t k m) d", d=DA_D), 16, DA_D, i, A,
                                     "summed", "mean")
                        v.wait_ge(A["root"], i + 1)
                        r = rstd[:].rearrange("p (t k m) -> p t k m", t=2, k=2)
                        for k, c0 in enumerate((DA_Q0, DA_K0)):
                            e = v.tensor_tensor(qn[:, :, k, :].rearrange("p t (m d) -> p t m d", d=DA_D),
                                                proj[:, :, ds(i * 256 + c0, 256)].rearrange("p t (m d) -> p t m d", d=DA_D),
                                                r[:, :, k, :].unsqueeze(3).to_broadcast([P, 2, 4, DA_D]), ALU.mult)
                        step(e, A["scaled"], i + 1)
                        for k in range(2):
                            q = qn[:, :, k, :].rearrange("p t (m d) -> p t m d", d=DA_D)
                            e = v.tensor_tensor(q, q, g_da[:, k, :].unsqueeze(1).unsqueeze(1).to_broadcast([P, 2, 4, DA_D]),
                                                ALU.mult)
                        step(e, A["gained"], i + 1)
                        q = qn[:].rearrange("p t k (m d) -> p t (k m) d", d=DA_D)
                        sin = trig[:, 0, :, 0:R1].unsqueeze(2).to_broadcast([P, 2, 8, R1])
                        cos = trig[:, 1, :, 0:R1].unsqueeze(2).to_broadcast([P, 2, 8, R1])
                        tv = tmp.rearrange("p n (t m d) -> p n t m d", t=2, m=8)
                        x1, x2 = q[:, :, :, 0:R1], q[:, :, :, R1:2 * R1]
                        v.tensor_tensor(tv[:, 0], x1, cos, ALU.mult)
                        v.tensor_tensor(tv[:, 1], x2, sin, ALU.mult)
                        v.tensor_tensor(tv[:, 2], x2, cos, ALU.mult)
                        step(v.tensor_tensor(tv[:, 3], x1, sin, ALU.mult), A["rprod"], i + 1)
                        v.tensor_tensor(x1, tv[:, 0], tv[:, 1], ALU.subtract)
                        v.tensor_tensor(x2, tv[:, 2], tv[:, 3], ALU.add).then_inc(A["rot"], 1)
                    if s == 5:
                        v.wait_ge(A["scored"], i + 1)
                        sd = at[:].rearrange("p b (h c) -> p b h c", h=2)[:, :, :, 0:P]
                        step(v.tensor_tensor(sd, sd, mask[:].unsqueeze(1).unsqueeze(1).to_broadcast([P, 4, 2, P]),
                                             ALU.add), A["masked"], i + 1)
                        v.tensor_reduce(mx[:, :, 0:1], at[:, :, 0:128], AX.X, ALU.max)
                        step(v.tensor_reduce(mx[:, :, 1:2], at[:, :, 128:384], AX.X, ALU.max), A["maxed"], i + 1)
                        v.tensor_scalar(nmx[:], mx[:], -DA_D ** -0.5, None, ALU.mult).then_inc(A["negmax"], 1)
                    if s == 7:
                        v.wait_ge(A["exped"], i + 1)
                        step(v.reciprocal(rden[:], den[:]), A["recip"], i + 1)
                        step(v.tensor_scalar(lrden[:], rden[:].rearrange("p (j m) t -> p j m t", m=2)[:, :, 1, :],
                                             neg_lam[:, 0:1], None, ALU.mult), A["lrecip"], i + 1)
                        spans = ((0, 128), (128, 384))
                        for j in range(2):
                            for t, (c0, c1) in enumerate(spans):
                                e = v.tensor_scalar(pm[:, 2 * j + 1, c0:c1], pm[:, 2 * j + 1, c0:c1],
                                                    lrden[:, j, t:t + 1], None, ALU.mult)
                        step(e, A["second"], i + 1)
                        for j in range(2):
                            for t, (c0, c1) in enumerate(spans):
                                e = v.scalar_tensor_tensor(out=pm[:, 2 * j, c0:c1], in0=pm[:, 2 * j, c0:c1],
                                                           scalar=rden[:, 2 * j, t:t + 1], in1=pm[:, 2 * j + 1, c0:c1],
                                                           op0=ALU.mult, op1=ALU.add)
                        e.then_inc(A["mixed"], 1)
                    if s == 10:
                        v.wait_ge(A["osq"], i + 1)
                        mean_squares(sq[:, :, 0, :].rearrange("p j (t d) -> p j t d", t=2), 4, DA_V, i, A,
                                     "osum", "omean")
                        v.wait_ge(A["oroot"], i + 1)
                        for j in range(2):
                            for t in range(TB):
                                n = 2 * j + t
                                e = v.scalar_tensor_tensor(out=osb[:, j, t * P:(t + 1) * P],
                                                           in0=at[:, 2 * j + 1, t * P:(t + 1) * P],
                                                           scalar=rstd[:, n:n + 1], in1=g_sub[:], op0=ALU.mult,
                                                           op1=ALU.mult)
                        e.then_inc(A["onorm"], 1)
                    if s == 11:
                        v.wait_ge(A["hi"], i + 1)
                        v.tensor_tensor(oT_lo[:, ds(i * 2 + 8, 2), :], at[:, 0, :].rearrange("p (a b) -> p a b", a=2),
                                        oT_hi[:, ds(i * 2 + 8, 2), :].bitcast(F32), ALU.subtract).then_inc(A["lo"], 1)
                    gated(i, s, U_MB, True, 0)
                    low(i * 12 + (G_MB + s), s)

            with v.Fori(0, 4) as i:
                for s in range(12):
                    if s == 0:
                        H = RT_D // 2
                        for t in range(TB):
                            qk = proj[:, t, RT_Q0:RT_V0].rearrange("p (k c) -> p k c", k=2)[:, :, ds(i * 128, 128)]
                            qk = qk.rearrange("p k (j d) -> p k j d", j=2)
                            x1, x2 = qk[:, :, :, 0:H], qk[:, :, :, H:2 * H]
                            sin = trig[:, 0, t, R1:NROT].unsqueeze(1).unsqueeze(1).to_broadcast([P, 2, 2, H])
                            cos = trig[:, 1, t, R1:NROT].unsqueeze(1).unsqueeze(1).to_broadcast([P, 2, 2, H])
                            tv = tmp.rearrange("p n (k j d) -> p n k j d", k=2, j=2)
                            dst = qn[:, t, :, 0:128].rearrange("p k (j d) -> p k j d", j=2)
                            v.tensor_tensor(tv[:, 0], x1, cos, ALU.mult)
                            v.tensor_tensor(tv[:, 1], x2, sin, ALU.mult)
                            v.tensor_tensor(tv[:, 2], x2, cos, ALU.mult)
                            step(v.tensor_tensor(tv[:, 3], x1, sin, ALU.mult), R["rprod"], i * 2 + (t + 1))
                            v.tensor_tensor(dst[:, :, :, 0:H], tv[:, 0], tv[:, 1], ALU.subtract)
                            step(v.tensor_tensor(dst[:, :, :, H:2 * H], tv[:, 2], tv[:, 3], ALU.add), R["rot"],
                                 i * 2 + (t + 1))
                    if s == 5:
                        v.wait_ge(R["scored"], i + 1)
                        v.wait_ge(R["decays"], i + 1)
                        for j in range(2):
                            for c0, c1 in ((0, 256), (256, 384)):
                                e = v.scalar_tensor_tensor(out=pm[:, j, c0:c1], in0=at[:, 1 + j, c0:c1],
                                                           scalar=RT_D ** -0.5, in1=dec[:, j, 0:c1 - c0],
                                                           op0=ALU.mult, op1=ALU.mult)
                        e.then_inc(R["weighed"], 1)
                    if s == 7:
                        v.wait_ge(R["tanh"], i + 1)
                        for t in range(TB):
                            e = v.scalar_tensor_tensor(out=tanh_g[:, t], in0=tanh_g[:, t], scalar=1.0,
                                               in1=proj[:, t, ds(i * 256 + RT_G0, 256)].rearrange(
                                                   "p (j d) -> p j d", j=2), op0=ALU.add,
                                               op1=ALU.mult)
                        e.then_inc(R["gmul"], 1)
                        v.wait_ge(R["osq"], i + 1)
                        mean_squares(sq[:, :, 0, :].rearrange("p t (j d) -> p t j d", j=2), 4, RT_V, i, R,
                                     "osum", "omean")
                        v.wait_ge(R["oroot"], i + 1)
                        for n in range(4):
                            e = v.scalar_tensor_tensor(out=osb[:, n // 2, (n % 2) * P:(n % 2 + 1) * P],
                                                       in0=at[:, 3, n * P:(n + 1) * P], scalar=rstd[:, n:n + 1],
                                                       in1=g_ret[:], op0=ALU.mult, op1=ALU.mult)
                        step(e, R["onorm"], i + 1)
                        v.wait_ge(R["gmul"], i + 1)
                        o4 = osb.rearrange("p t (j d) -> p t j d", j=2)
                        v.tensor_tensor(o4, o4, tanh_g, ALU.mult).then_inc(R["gated"], 1)
                    if s == 10:
                        v.wait_ge(R["hi"], i + 1)
                        v.tensor_tensor(oT_lo[:, ds(i * 2, 2), :], at[:, 0, :].rearrange("p (a b) -> p a b", a=2),
                                        oT_hi[:, ds(i * 2, 2), :].bitcast(F32), ALU.subtract).then_inc(R["lo"], 1)
                    gated(i, s, U_DB, False, 0)
                    low(i * 12 + (G_DB + s), s)

            with v.Fori(0, 4) as i:
                for s in range(12):
                    gated(i, s, U_RB, False, 4)
                    low(i * 12 + (G_RB + s), s)

            low_columns(2 * KD, oT_lo, oT_hi, lambda k: 0.5)

            def residual(u, p, dst, count):
                v.wait_ge(acc_ready[p], u + 1)
                v.tensor_tensor(dst, acc[p][:], dst, ALU.add).then_inc(acc_free[p], 1)
                v.wait_ge(acc_free[p], u + 2)
                v.nop().then_inc(x2_done, 1)

            v.wait_ge(x_again, 32)
            with v.Fori(0, 2) as i:
                for s in range(16):
                    if s in (7, 15):
                        p = s // 8
                        residual(i + U_OUT, p, proj[:, :, ds(i * 1024 + p * NCOL, NCOL)], None)
                    low(i * 16 + (G_OUT + s), s)
            scale_rows(2, proj, proj, 0, D)
            low_columns(3 * KD, hT_lo, hT_hi, lambda k: g_cols[:, 2 * KD + k:2 * KD + k + 1])

            def activations(u, f):
                v.wait_ge(acc_ready[1], u + 1)
                v.wait_ge(acc_free[0], u + 2)
                if not isinstance(f, int):
                    v.wait_ge(ff_ps, f)
                v.tensor_tensor(gt, acc[1][:], sg, ALU.mult).then_inc(acc_free[1], 1)
                v.wait_ge(acc_free[1], u + 2)
                v.nop().then_inc(ff_act, 1)

            def low_acts(f):
                v.wait_ge(ff_hi, f)
                v.tensor_tensor(oT_lo[:, 0:4, :], at[:, 0:2, :].rearrange("p b (a c) -> p (b a) c", a=2),
                                oT_hi[:, 0:4, :].bitcast(F32), ALU.subtract).then_inc(ff_lo, 1)

            for s in range(16):
                if s == 15:
                    activations(U_F0, 0)
                low(G_F0 + s, s)
            with v.Fori(1, NF) as f:
                for s in range(24):
                    if s == 3:
                        low_acts(f)
                    if s == 15:
                        activations(f * 3 + (U_F - 3), f)
                    if s in (17, 19, 21, 23):
                        n = (s - 17) // 2
                        residual(f * 3 + (U_F - 3 + 1 + n // 2), n % 2, proj[:, :, n * NCOL:(n + 1) * NCOL], None)
                    low(f * 24 + (G_F - 24 + s), s)
            low_acts(NF)
            for s in range(8):
                if s % 2 == 1:
                    n = s // 2
                    residual(U_END + n // 2, n % 2, proj[:, :, n * NCOL:(n + 1) * NCOL], None)
                if s < 4:
                    low(G_END + s, s)

        @block.tensor
        def _(pe):
            def pair(g, s, hi, lo, k0, p, first, last, col=None):
                pe.wait_ge(lo_done, g + 1)
                if col is not None:
                    pe.wait_ge(col_lo, col)
                for k in range(2):
                    for t in range(TB):
                        tok = slice(t * P, (t + 1) * P)
                        terms = ((hi, w_hi), (hi, w_lo), (lo, w_hi))
                        for n, (a, w) in enumerate(terms):
                            e = pe.matmul(acc[p][:, t, :], a[:, k0 + k, tok], w[:, s % RING, k, :],
                                          start=first and k == 0 and n == 0, stop=last and k == 1 and n == 2)
                return e

            def chunk_pair(g, s, hi, lo, k0, kk, nk, u, p, col=None):
                if kk == 0:
                    pe.wait_ge(acc_free[p], u + 1)
                e = pair(g, s, hi, lo, k0 + 2 * kk, p, kk == 0, kk == nk - 1, col)
                e.then_inc(pair_used, 1)
                if kk == nk - 1:
                    pe.wait_ge(pair_used, g + 1)
                    pe.nop().then_inc(acc_ready[p], 1)

            def turn(out, src):
                return pe.transpose(out, src, ident[:])

            def turn_columns(n0, src, c0, row=None):
                for k in range(KD):
                    if n0 + k >= 4:
                        pe.wait_ge(col_lo, n0 + k - 3)
                    for t in range(TB):
                        if row is not None and k == 0:
                            pe.wait_ge(row_ok, row + t + 1)
                        e = turn(at[:, k % 4, t * P:(t + 1) * P], src[:, t, c0 + k * P:c0 + (k + 1) * P])
                    e.then_inc(col_ps, 1)

            pe.wait_ge(const_in, 16 * 15)
            pe.wait_ge(masks, 3)
            pe.transpose(at[:, 3, 0:3 * KD], g_rows, ident[0:3 * KD, 0:3 * KD]).then_inc(gcol_ps, 1)
            pe.wait_ge(gcol_ok, 1)
            turn_columns(0, proj, 0, 0)
            for s in range(16):
                chunk_pair(G_KV + s, s, oT_hi, oT_lo, 0, s % 8, 8, U_KV, s // 8, 2 * s + 2 if s < 8 else None)
            with pe.Fori(1, 2) as i:
                for s in range(16):
                    chunk_pair(i * 16 + (G_KV + s), s, oT_hi, oT_lo, 0, s % 8, 8, i + U_KV, s // 8)
            turn_columns(KD, proj, D, 2)
            for s in range(16):
                chunk_pair(G_MQ + s, s, hT_hi, hT_lo, 0, s % 8, 8, U_MQ, s // 8, KD + 2 * s + 2 if s < 8 else None)

            with pe.Fori(0, MEM_H) as i:
                for s in range(16):
                    chunk_pair(i * 16 + (G_PROJ + s), s, hT_hi, hT_lo, 0, s % 8, 8, i + U_PROJ, s // 8)
                    if s == 2:
                        pe.wait_ge(M["normed"], i + 1)
                        for k in range(2):
                            for h in range(2):
                                for t in range(TB):
                                    e = turn(at[:, k, h * 256 + t * P:h * 256 + (t + 1) * P],
                                             qn[:, t, k, h * P:(h + 1) * P])
                        e.then_inc(M["turned"], 1)
                    if s == 4:
                        pe.wait_ge(M["copied"], i + 1)
                        for t in range(TB):
                            for h in range(2):
                                e = pe.matmul(at[:, 2, t * 256:(t + 1) * 256],
                                              qkT[:, 0, h * 256 + t * P:h * 256 + (t + 1) * P],
                                              qkT[:, 1, h * 256:(h + 1) * 256], start=h == 0, stop=h == 1)
                        e.then_inc(M["scored"], 1)
                    if s == 6:
                        pe.wait_ge(M["exped"], i + 1)
                        for k in range(2):
                            for t in range(TB):
                                e = turn(at[:, 3, k * 256 + t * P:k * 256 + (t + 1) * P], pm[:, t, k * P:(k + 1) * P])
                        e.then_inc(M["pT_ps"], 1)
                    if s == 8:
                        pe.wait_ge(M["pT"], i + 1)
                        for t in range(TB):
                            for k in range(2):
                                e = pe.matmul(at[:, 0, t * 256:(t + 1) * 256], pT[:, k, t * P:(t + 1) * P],
                                              kvm[:, k, ds(i * MEM_D + 1024, MEM_D)], start=k == 0, stop=k == 1)
                        e.then_inc(M["ov"], 1)
                    if s == 10:
                        pe.wait_ge(M["onorm"], i + 1)
                        for h in range(2):
                            for t in range(TB):
                                e = turn(at[:, 1, h * 256 + t * P:h * 256 + (t + 1) * P], osb[:, t, h * P:(h + 1) * P])
                        e.then_inc(M["oT_ps"], 1)
            with pe.Fori(0, 2) as i:
                for s in range(16):
                    chunk_pair(i * 16 + (G_PROJ + 64 + s), s, hT_hi, hT_lo, 0, s % 8, 8, i + (U_PROJ + 4), s // 8)

            def gate_branch(i, s, g0, u0, k0):
                if s < 8:
                    chunk_pair(i * 12 + (g0 + s), s, hT_hi, hT_lo, 0, s, 8, i + u0, 0)
                else:
                    chunk_pair(i * 12 + (g0 + s), s, oT_hi, oT_lo, k0, s - 8, 4, i + u0, 1)

            pe.wait_ge(M["lo"], MEM_H)
            with pe.Fori(0, 4) as i:
                for s in range(12):
                    gate_branch(i, s, G_MB, U_MB, 0)
                    if s == 2:
                        pe.wait_ge(A["rot"], i + 1)
                        for j in range(2):
                            for k in range(2):
                                for t in range(TB):
                                    e = turn(at[:, 2 * j, k * 256 + t * P:k * 256 + (t + 1) * P],
                                             qn[:, t, k, j * P:(j + 1) * P])
                        e.then_inc(A["turned"], 1)
                    if s == 4:
                        pe.wait_ge(A["copied"], i + 1)
                        for j in range(2):
                            for m in range(2):
                                row = slice(m * DA_D, (m + 1) * DA_D)
                                pe.matmul(at[:, 2 * j + m, 0:128], qkT[row, j, 0:128], qkT[row, j, 256:384],
                                          start=True, stop=True)
                                e = pe.matmul(at[:, 2 * j + m, 128:384], qkT[row, j, 128:256],
                                              qkT[row, j, 256:512], start=True, stop=True)
                        e.then_inc(A["scored"], 1)
                    if s == 8:
                        pe.wait_ge(A["mixed"], i + 1)
                        for j in range(2):
                            for n in range(3):
                                e = turn(at[:, 2 * j, n * P:(n + 1) * P], pm[:, 2 * j, n * P:(n + 1) * P])
                        e.then_inc(A["pT_ps"], 1)
                    if s == 9:
                        pe.wait_ge(A["pT"], i + 1)
                        for j in range(2):
                            v0 = proj[:, 0, ds(i * 256 + (DA_V0 + j * P), P)]
                            v1 = proj[:, 1, ds(i * 256 + (DA_V0 + j * P), P)]
                            pe.matmul(at[:, 2 * j + 1, 0:128], pT[:, j, 0:128], v0, start=True, stop=True)
                            pe.matmul(at[:, 2 * j + 1, 128:256], pT[:, j, 128:256], v0, start=True, stop=False)
                            e = pe.matmul(at[:, 2 * j + 1, 128:256], pT[:, j, 256:384], v1, start=False, stop=True)
                        e.then_inc(A["ov"], 1)
                    if s == 11:
                        pe.wait_ge(A["onorm"], i + 1)
                        for j in range(2):
                            for t in range(TB):
                                e = turn(at[:, 0, j * 256 + t * P:j * 256 + (t + 1) * P], osb[:, j, t * P:(t + 1) * P])
                        e.then_inc(A["oT_ps"], 1)

            pe.wait_ge(A["lo"], 4)
            with pe.Fori(0, 4) as i:
                for s in range(12):
                    gate_branch(i, s, G_DB, U_DB, 8)
                    if s == 2:
                        pe.wait_ge(R["rot"], i * 2 + 2)
                        for k in range(2):
                            for t in range(TB):
                                e = turn(at[:, 0, k * 256 + t * P:k * 256 + (t + 1) * P], qn[:, t, k, 0:128])
                        e.then_inc(R["turned"], 1)
                    if s == 4:
                        pe.wait_ge(R["copied"], i + 1)
                        for j in range(2):
                            row = slice(j * RT_D, (j + 1) * RT_D)
                            pe.matmul(at[:, 1 + j, 0:256], qkT[row, 0, 256:384], qkT[row, 0, 0:256],
                                      start=True, stop=True)
                            e = pe.matmul(at[:, 1 + j, 256:384], qkT[row, 0, 384:512], qkT[row, 0, 128:256],
                                          start=True, stop=True)
                        e.then_inc(R["scored"], 1)
                    if s == 6:
                        pe.wait_ge(R["weighed"], i + 1)
                        for j in range(2):
                            v0 = proj[:, 0, ds(i * 256 + (RT_V0 + j * P), P)]
                            v1 = proj[:, 1, ds(i * 256 + (RT_V0 + j * P), P)]
                            o0, o1 = at[:, 3, j * P:(j + 1) * P], at[:, 3, 256 + j * P:256 + (j + 1) * P]
                            pe.matmul(o0, pm[:, j, 0:128], v0, start=True, stop=True)
                            pe.matmul(o1, pm[:, j, 128:256], v0, start=True, stop=False)
                            e = pe.matmul(o1, pm[:, j, 256:384], v1, start=False, stop=True)
                        e.then_inc(R["ov"], 1)
                    if s == 9:
                        pe.wait_ge(R["gated"], i + 1)
                        for j in range(2):
                            for t in range(TB):
                                e = turn(at[:, 0, j * 256 + t * P:j * 256 + (t + 1) * P], osb[:, t, j * P:(j + 1) * P])
                        e.then_inc(R["oT_ps"], 1)

            pe.wait_ge(R["lo"], 4)
            with pe.Fori(0, 4) as i:
                for s in range(12):
                    gate_branch(i, s, G_RB, U_RB, 0)

            pe.wait_ge(merged, 8)
            turn_columns(2 * KD, kvm, 0)
            for s in range(16):
                chunk_pair(G_OUT + s, s, oT_hi, oT_lo, 0, s % 8, 8, U_OUT, s // 8, 2 * KD + 2 * s + 2 if s < 8 else None)
            with pe.Fori(1, 2) as i:
                for s in range(16):
                    chunk_pair(i * 16 + (G_OUT + s), s, oT_hi, oT_lo, 0, s % 8, 8, i + U_OUT, s // 8)
            turn_columns(3 * KD, proj, D, 4)

            def turn_acts(f):
                pe.wait_ge(ff_act, f)
                for k in range(4):
                    for t in range(TB):
                        c0 = (k % 2) * 256 + t * P
                        e = turn(at[:, k // 2, c0:c0 + P], gt[:, t, k * P:(k + 1) * P])
                e.then_inc(ff_ps, 1)

            for s in range(16):
                chunk_pair(G_F0 + s, s, hT_hi, hT_lo, 0, s % 8, 8, U_F0, s // 8, 3 * KD + 2 * s + 2 if s < 8 else None)
            with pe.Fori(1, NF) as f:
                for s in range(24):
                    g, u = f * 24 + (G_F - 24 + s), f * 3 + (U_F - 3)
                    if s < 16:
                        chunk_pair(g, s, hT_hi, hT_lo, 0, s % 8, 8, u, s // 8)
                    else:
                        if s == 16:
                            pe.wait_ge(ff_lo, f)
                        n = (s - 16) // 2
                        chunk_pair(g, s, oT_hi, oT_lo, 0, s % 2, 2, u + (1 + n // 2), n % 2)
                    if s == 2:
                        turn_acts(f)
            turn_acts(NF)
            pe.wait_ge(ff_lo, NF)
            for s in range(8):
                chunk_pair(G_END + s, s, oT_hi, oT_lo, 0, s % 2, 2, U_END + s // 4, (s // 2) % 2)


_INS = ['x', 'mem', 'positions', 'attn_norm_g', 'w_in', 'da_q_norm_g', 'da_k_norm_g', 'da_lambda_q1', 'da_lambda_k1',
        'da_lambda_q2', 'da_lambda_k2', 'da_subln_g', 'ret_norm_g', 'mem_norm_g', 'w_mem_kv', 'mem_q_norm_g',
        'mem_k_norm_g', 'w_o_da', 'w_o_ret', 'w_o_mem', 'w_out', 'ffn_norm_g', 'w_ffn_gate', 'w_ffn_up', 'w_ffn_down']


def kernel(**inputs):
    import concourse.bacc as _bacc
    from concourse.bass_utils import run_bass_kernel_spmd as _run

    nc = _bacc.Bacc("TRN2", target_bir_lowering=False, num_devices=1)
    arrays, args = {}, []
    for name in _INS + ["shape_consts"]:
        a = shape_constants() if name == "shape_consts" else np.ascontiguousarray(inputs[name])
        arrays[f"in_{name}"] = a
        args.append(nc.dram_tensor(f"in_{name}", a.shape, mybir.dt.from_np(a.dtype), kind="ExternalInput").ap())
    args.append(nc.dram_tensor("out_0", (1, TOK, D), F32, kind="ExternalOutput").ap())
    program(nc, *args)
    r = _run(nc, [arrays], core_ids=[0])
    return r.results[0]["out_0"]
```

```python
from contextlib import ExitStack

import numpy as np

import concourse.bass as bass
from concourse import mybir

F32 = mybir.dt.float32
F32R = mybir.dt.float32r
I32 = mybir.dt.int32
ALU = mybir.AluOpType
ACT = mybir.ActivationFunctionType
AX = mybir.AxisListType

P = 128
D = 2048
TB = 2
TOK = TB * P
NCOL = 512
KD = D // P
EPS = 1e-6
LAMBDA_INIT = 0.2

DA_H, DA_D, DA_V, DA_ROT = 8, 64, 128, 16
RT_H, RT_D, RT_V = 8, 64, 128
MEM_H, MEM_D = 4, 256
DA_THETA, RT_THETA = 500000.0, 10000.0
D_FF = 5632
NF = D_FF // NCOL

DA_Q0, DA_K0, DA_V0 = 0, 1024, 2048
RT_Q0, RT_K0, RT_V0, RT_G0 = 3072, 3584, 4096, 5120
MQ0, GATE0 = 6144, 7168
GATE_DA, GATE_RT, GATE_MEM = GATE0, GATE0 + D, GATE0 + 2 * D

RING = 4
G_KV, G_MQ, G_PROJ, G_MB, G_DB, G_RB, G_OUT, G_F0, G_F = 0, 32, 48, 144, 192, 240, 288, 320, 336
G_END = G_F + 24 * (NF - 1)
PAIRS = G_END + 8
U_KV, U_MQ, U_PROJ, U_MB, U_DB, U_RB, U_OUT, U_F0, U_F = 0, 2, 3, 9, 13, 17, 21, 23, 24
U_END = U_F + 3 * (NF - 1)
NEG = -1.0e30
FAR = 3.0e7
TWO_PI = (6.28125, 0.0019350051879882812, 3.019916050173085e-07)
ROUND = 12582912.0


def shape_constants():
    da = np.float32(DA_THETA) ** (-np.arange(DA_ROT // 2, dtype=np.float32) * np.float32(2.0) / np.float32(DA_ROT))
    rt = np.float32(RT_THETA) ** (-np.arange(RT_D // 2, dtype=np.float32) * np.float32(2.0) / np.float32(RT_D))
    lg = np.log(np.float32(1.0) - np.float32(2.0) ** (np.float32(-5.0) - np.arange(RT_H, dtype=np.float32)))
    return np.concatenate([da, rt, lg]).astype(np.float32)[None, :]


def program(nc, x, mem, positions, attn_norm_g, w_in, da_q_norm_g, da_k_norm_g, da_lambda_q1, da_lambda_k1,
            da_lambda_q2, da_lambda_k2, da_subln_g, ret_norm_g, mem_norm_g, w_mem_kv, mem_q_norm_g,
            mem_k_norm_g, w_o_da, w_o_ret, w_o_mem, w_out, ffn_norm_g, w_ffn_gate, w_ffn_up, w_ffn_down,
            shape_consts, out):
    ds = bass.ds
    NROT = DA_ROT // 2 + RT_D // 2
    R1 = DA_ROT // 2
    with ExitStack() as ctx:
        def sb(name, shape, dt=F32):
            return ctx.enter_context(nc.sbuf_tensor(name, shape, dt))

        def sem(name):
            return ctx.enter_context(nc.semaphore(name))

        raw = sb("raw", [P, RING, 2, NCOL])
        w_hi = sb("w_hi", [P, RING, 2, NCOL], F32R)
        w_lo = sb("w_lo", [P, RING, 2, NCOL], F32R)
        hT_hi = sb("hT_hi", [P, KD, TOK], F32R)
        hT_lo = sb("hT_lo", [P, KD, TOK], F32R)
        oT_hi = sb("oT_hi", [P, KD, TOK], F32R)
        oT_lo = sb("oT_lo", [P, KD, TOK], F32R)
        proj = sb("proj", [P, TB, GATE0])
        kvm = sb("kvm", [P, TB, D])
        sq = sb("sq", [P, TB, 2, 256])
        qn = sb("qn", [P, TB, 2, 256])
        pm = sb("pm", [P, 4, 384])
        ident = sb("ident", [P, P])
        mask = sb("mask", [P, P])
        rel = sb("rel", [P, 256])
        g_cols = sb("g_cols", [P, 3 * KD])
        g_da = sb("g_da", [P, 2, DA_D])
        g_mem = sb("g_mem", [P, 2, MEM_D])
        g_sub = sb("g_sub", [P, DA_V])
        g_ret = sb("g_ret", [P, RT_V])
        lam_s = sb("lam_s", [P, 2])
        lam_e = sb("lam_e", [P, 2])
        neg_lam = sb("neg_lam", [P, 1])
        sc = sb("sc", [P, NROT + RT_H])
        pos_i = sb("pos_i", [P, TB], I32)
        pos_f = sb("pos_f", [P, TB])
        trig = sb("trig", [P, 2, TB, NROT])
        minus_half = sb("minus_half", [P, 16])
        ss = sb("ss", [P, 16])
        ms = sb("ms", [P, 16])
        rstd = sb("rstd", [P, 16])
        row_ss = sb("row_ss", [P, 3, TB])
        x2_ss = sb("x2_ss", [P, TB, 4])
        half_rstd = sb("half_rstd", [P, TB])
        row_ms = sb("row_ms", [P, 3, TB])
        row_rstd = sb("row_rstd", [P, 3, TB])
        mx = sb("mx", [P, 4, 2])
        nmx = sb("nmx", [P, 4, 2])
        den = sb("den", [P, 4, 2])
        rden = sb("rden", [P, 4, 2])
        lrden = sb("lrden", [P, 2, 2])

        sq_flat, qn_flat, pm_flat = (a[:].rearrange(r) for a, r in (
            (sq, "p t k d -> p (t k d)"), (qn, "p t k d -> p (t k d)"), (pm, "p b c -> p (b c)")))
        qkT = sq_flat.rearrange("p (j c) -> p j c", j=2)
        pT = qn_flat[:, 0:768].rearrange("p (j c) -> p j c", j=2)
        osb = pm_flat[:, 0:512].rearrange("p (a c) -> p a c", a=2)
        tmp = pm_flat[:, 0:512].rearrange("p (n c) -> p n c", n=4)
        tmp2 = pm_flat[:, 768:1280].rearrange("p (n c) -> p n c", n=4)
        v_head = pm_flat[:, 768:1280].rearrange("p (k d) -> p k d", k=2)
        dec = pm_flat[:, 768:1280].rearrange("p (j c) -> p j c", j=2)
        tanh_g = qn[:, :, :, P:2 * P]
        lam_in = pm_flat[:, 0:256].rearrange("p (a b d) -> p a b d", a=2, b=2)
        lam_pr = pm_flat[:, 256:384].rearrange("p (b d) -> p b d", b=2)
        ang = pm_flat[:, 384:544].rearrange("p (k t n) -> p k t n", k=2, t=TB)
        turns = pm_flat[:, 544:704].rearrange("p (k t n) -> p k t n", k=2, t=TB)
        g_rows = pm_flat[0:3 * KD, 768:768 + P]
        gt = proj[:, :, MQ0:MQ0 + NCOL]
        sg = proj[:, :, MQ0 + NCOL:MQ0 + 2 * NCOL]

        acc = [ctx.enter_context(nc.psum_tensor(f"acc{i}", [P, TB, NCOL], F32)) for i in range(2)]
        at = ctx.enter_context(nc.psum_tensor("at", [P, 4, 512], F32))

        loaded = [sem(f"loaded{i}") for i in range(RING)]
        hi_done, lo_done = sem("hi_done"), sem("lo_done")
        pair_used = sem("pair_used")
        acc_free = [sem(f"acc_free{i}") for i in range(2)]
        mem_in, x_in = [sem(f"mem_in{i}") for i in range(4)], [sem(f"x_in{i}") for i in range(2)]
        x_again = sem("x_again")
        const_in = sem("const_in")
        rows_in = sem("rows_in")
        zeroed, masks = sem("zeroed"), sem("masks")
        gcol_ps, gcol_ok = sem("gcol_ps"), sem("gcol_ok")
        row_sq, row_sum, row_mean, row_root = sem("row_sq"), sem("row_sum"), sem("row_mean"), sem("row_root")
        row_half = sem("row_half")
        col_ps, col_hi, col_lo = sem("col_ps"), sem("col_hi"), sem("col_lo")
        setup_v, setup_a = sem("setup_v"), sem("setup_a")
        end_done, end_added = sem("end_done"), sem("end_added")
        out_done = sem("out_done")

        def phase_sems(tag, names):
            return {n: sem(f"{tag}_{n}") for n in names}
        M = phase_sems("mem", "squared summed mean root normed values turned copied scored maxed negmax exped recip "
                              "weighed pT_ps pT ov hi lo".split())
        A = phase_sems("da", "squared summed mean root scaled gained rprod rot turned copied scored masked maxed negmax "
                             "exped recip lrecip second mixed pT_ps pT ov osq osum omean oroot onorm oT_ps hi lo".split())
        R = phase_sems("ret", "decays tanh rprod rot turned copied scored weighed ov osq osum omean oroot onorm gmul "
                              "gated oT_ps hi lo".split())
        merged = sem("merged")
        ff_ps, ff_hi, ff_lo = sem("ff_ps"), sem("ff_hi"), sem("ff_lo")

        block = ctx.enter_context(nc.Block())

        def tiles(w, row0, col0):
            return w[ds(row0, 2 * P), ds(col0, NCOL)].rearrange("(k p) n -> p k n", p=P)

        w_in2, w_kv2, w_out2 = w_in[0], w_mem_kv[0], w_out[0]
        w_g2, w_u2, w_d2 = w_ffn_gate[0], w_ffn_up[0], w_ffn_down[0]

        @block.sync
        def _(sp):
            def load(w, row0, col0, g, s):
                if not (isinstance(g, int) and g < RING):
                    sp.wait_ge(lo_done, g - RING + 1)
                sp.dma_start(raw[:, s % RING], tiles(w, row0, col0)).then_inc(loaded[s % RING], 16)

            def load_chunk(w, row0, col0, g, s, n=KD // 2):
                for k in range(n):
                    load(w, row0 + 2 * P * k, col0, g + k, s + k)

            def const(dst, src, done):
                sp.dma_start(dst, src).then_inc(done, 16)

            def gain_row(k, g):
                const(g_rows[k * KD:(k + 1) * KD, :], g[0].rearrange("(k p) -> k p", p=P), rows_in)

            for k in range(4):
                cols = slice(k * NCOL, (k + 1) * NCOL)
                sp.dma_start(proj[:, :, cols], mem[0].rearrange("(t p) n -> p t n", p=P)[:, :, cols]).then_inc(mem_in[k], 16)
                if k == 0:
                    gain_row(0, mem_norm_g)
                load(w_kv2, 2 * P * k, 0, k, k)
                if k == 0:
                    gain_row(1, attn_norm_g)
                    gain_row(2, ffn_norm_g)
            for t in range(TB):
                sp.dma_start(proj[:, t, D:2 * D], x[0, t * P:(t + 1) * P, :]).then_inc(x_in[t], 16)
            for k in range(4, 8):
                load(w_kv2, 2 * P * k, 0, k, k)
            for dst, src in ((g_da[:, 0], da_q_norm_g), (g_da[:, 1], da_k_norm_g), (g_mem[:, 0], mem_q_norm_g),
                             (g_mem[:, 1], mem_k_norm_g), (g_sub[:], da_subln_g), (g_ret[:], ret_norm_g),
                             (lam_in[:, 0, 0], da_lambda_q1), (lam_in[:, 0, 1], da_lambda_q2),
                             (lam_in[:, 1, 0], da_lambda_k1), (lam_in[:, 1, 1], da_lambda_k2), (sc[:], shape_consts)):
                const(dst, src[0].partition_broadcast(P), const_in)
            with nc.allow_non_contiguous_dma(reason="256 positions, once"):
                const(pos_i[:], positions[0].rearrange("(t p) -> p t", p=P), const_in)
            with sp.Fori(1, 4) as n:
                load_chunk(w_kv2, 0, n * NCOL, G_KV + n * 8, 0)
            with sp.Fori(0, 2) as n:
                load_chunk(w_in2, 0, n * NCOL + MQ0, n * 8 + G_MQ, 0)
            with sp.Fori(0, 12) as n:
                load_chunk(w_in2, 0, n * NCOL, n * 8 + G_PROJ, 0)
            for gate, wo, g0 in ((GATE_MEM, w_o_mem, G_MB), (GATE_DA, w_o_da, G_DB), (GATE_RT, w_o_ret, G_RB)):
                with sp.Fori(1, 5) as n:
                    load_chunk(w_in2, 0, n * NCOL + (gate - NCOL), n * 12 + (g0 - 12), 0)
                    load_chunk(wo[0], 0, n * NCOL - NCOL, n * 12 + (g0 - 4), 8, 4)
                if gate == GATE_DA:
                    sp.wait_ge(A["lo"], 4)
                    for t in range(TB):
                        sp.dma_start(proj[:, t, 0:D], x[0, t * P:(t + 1) * P, :]).then_inc(x_again, 16)
            with sp.Fori(0, 4) as n:
                load_chunk(w_out2, 0, n * NCOL, n * 8 + G_OUT, 0)
            load_chunk(w_g2, 0, 0, G_F0, 0)
            load_chunk(w_u2, 0, 0, G_F0 + 8, 8)
            with sp.Fori(1, NF) as f:
                g0 = f * 24 + (G_F - 24)
                load_chunk(w_g2, 0, f * NCOL, g0, 0)
                load_chunk(w_u2, 0, f * NCOL, g0 + 8, 8)
                for n in range(4):
                    load_chunk(w_d2, f * NCOL - NCOL, n * NCOL, g0 + (16 + 2 * n), 2 * n, 2)
            for n in range(4):
                load_chunk(w_d2, (NF - 1) * NCOL, n * NCOL, G_END + 2 * n, 2 * n, 2)
            for n in range(3):
                sp.wait_ge(acc_free[n % 2], U_END + n // 2 + 2)
                sp.dma_start(out[0].rearrange("(t p) n -> p t n", p=P)[:, :, n * NCOL:(n + 1) * NCOL],
                             proj[:, :, n * NCOL:(n + 1) * NCOL]).then_inc(out_done, 16)
            for t in range(TB):
                sp.wait_ge(end_added, t + 1)
                sp.dma_start(out[0, t * P:(t + 1) * P, D - NCOL:D], proj[:, t, D - NCOL:D]).then_inc(out_done, 16)
            sp.wait_ge(out_done, 16 * 5)

        @block.gpsimd
        def _(pool):
            nc.gpsimd.memset(ident[:], 0.0).then_inc(zeroed, 1)
            nc.gpsimd.memset(mask[:], 0.0).then_inc(zeroed, 1)
            nc.gpsimd.memset(minus_half[:], -0.5).then_inc(zeroed, 1)
            nc.gpsimd.iota(rel[:], pattern=[[1, 256]], base=0, channel_multiplier=-1,
                           allow_small_or_imprecise_dtypes=True).then_inc(zeroed, 1)
            pool.wait_ge(zeroed, 4)
            nc.gpsimd.affine_select(out=ident[:], in_=ident[:], compare_op=ALU.not_equal, fill=1.0, base=0,
                                    pattern=[[-1, P]], channel_multiplier=1).then_inc(masks, 1)
            nc.gpsimd.affine_select(out=mask[:], in_=mask[:], compare_op=ALU.is_ge, fill=NEG, base=0,
                                    pattern=[[-1, P]], channel_multiplier=1).then_inc(masks, 1)
            nc.gpsimd.affine_select(out=rel[:], in_=rel[:], compare_op=ALU.is_ge, fill=FAR, base=0,
                                    pattern=[[1, 256]], channel_multiplier=-1).then_inc(masks, 1)

            def row_roots(k):
                for t in range(TB):
                    pool.wait_ge(row_mean, 2 * k + t + 1 if k < 2 else 5)
                    nc.gpsimd.tensor_tensor(row_rstd[:, k, t:t + 1], row_ms[:, k, t:t + 1], minus_half[:, 0:1],
                                            ALU.pow).then_inc(row_root, 1)

            def head_roots(ready, done, i, n):
                pool.wait_ge(ready, i + 1)
                nc.gpsimd.tensor_tensor(rstd[:, 0:n], ms[:, 0:n], minus_half[:, 0:n], ALU.pow).then_inc(done, 1)

            row_roots(0)
            row_roots(1)
            with pool.Fori(0, MEM_H) as i:
                head_roots(M["mean"], M["root"], i, 4)
            with pool.Fori(0, 4) as i:
                head_roots(A["mean"], A["root"], i, 16)
                head_roots(A["omean"], A["oroot"], i, 4)
            with pool.Fori(0, 4) as i:
                head_roots(R["omean"], R["oroot"], i, 4)
            row_roots(2)

        @block.scalar
        def _(act):
            def high(g, s):
                act.wait_ge(loaded[s % RING], (g // RING + 2) * 16 if isinstance(g, int) else g * 4 + (32 - 4 * (s % RING)))
                act.wait_ge(pair_used, g + 1)
                act.activation(w_hi[:, s % RING], raw[:, s % RING], ACT.Copy).then_inc(hi_done, 1)

            def row_squares(k, ready, src, col0):
                for t in range(TB):
                    act.wait_ge(*ready(t))
                    if k == 1:
                        act.wait_ge(row_sq, t + 1)
                    act.activation(kvm[:, t, :], src[:, t, col0:col0 + D], ACT.Square,
                                   accum_out=row_ss[:, k, t:t + 1]).then_inc(row_sq, 1)

            def high_columns(n0, ks, dst, scale, shift=0):
                for k in ks:
                    act.wait_ge(col_ps, n0 + k + 1)
                    act.activation(dst[:, (k + shift) % KD, :], at[:, k % 4, 0:TOK], ACT.Copy,
                                   scale=scale(k)).then_inc(col_hi, 1)

            def evacuate(g, p, norm, dst):
                act.wait_ge(pair_used, g + 1)
                for t in range(TB):
                    e = act.activation(dst[:, t], acc[p][:, t, :], ACT.Copy, scale=row_rstd[:, norm, t:t + 1])
                e.then_inc(acc_free[p], 1)

            act.wait_ge(zeroed, 4)
            act.activation(nmx[:, 0, 0:1], minus_half[:, 0:1], ACT.Copy)
            act.wait_ge(gcol_ok, 1)
            high_columns(0, range(2), oT_hi, lambda k: g_cols[:, k:k + 1])
            for s in range(RING):
                act.wait_ge(loaded[s], 16)
                act.activation(w_hi[:, s], raw[:, s], ACT.Copy).then_inc(hi_done, 1)
                high_columns(0, range(2 + 2 * s, 4 + 2 * s), oT_hi, lambda k: g_cols[:, k:k + 1])
            high_columns(0, range(10, KD), oT_hi, lambda k: g_cols[:, k:k + 1])

            def memory_kv(i, s):
                if s in (7, 15):
                    if s == 7:
                        act.wait_ge(row_root, 2)
                        act.wait_ge(row_sq, 4)
                    evacuate(i * 16 + (G_KV + s), s // 8, 0, kvm[:, :, ds(i * 1024 + (s // 8) * NCOL, NCOL)])
                high(i * 16 + (G_KV + s), s)

            for s in range(16):
                if s == 2:
                    for k in range(3):
                        act.wait_ge(mem_in[k], 16)
                    row_squares(0, lambda t: (mem_in[3], 16), proj, 0)
                if s == 5:
                    row_squares(1, lambda t: (x_in[t], 16), proj, D)
                if s >= 8:
                    high_columns(KD, range(2 * s - 16, 2 * s - 14), hT_hi, lambda k: g_cols[:, KD + k:KD + k + 1])
                memory_kv(0, s)
            with act.Fori(1, 2) as i:
                for s in range(16):
                    memory_kv(i, s)

            act.wait_ge(row_root, 4)
            for s in range(16):
                if s == 4:
                    act.wait_ge(setup_v, 11)
                    act.activation(trig[:], ang, ACT.Sin).then_inc(setup_a, 1)
                    act.activation(lam_e[:], lam_s[:], ACT.Exp).then_inc(setup_a, 1)
                if s in (7, 15):
                    c0 = MQ0 + (s // 8) * NCOL
                    evacuate(G_MQ + s, s // 8, 1, proj[:, :, c0:c0 + NCOL])
                high(G_MQ + s, s)

            def projections(i, s, i0):
                if s in (7, 15):
                    evacuate(i * 16 + (G_PROJ + 16 * i0 + s), s // 8, 1,
                             proj[:, :, ds(i * 1024 + (1024 * i0 + (s // 8) * NCOL), NCOL)])
                high(i * 16 + (G_PROJ + 16 * i0 + s), s)

            with act.Fori(0, MEM_H) as i:
                for s in range(16):
                    if s == 0:
                        act.activation(sq[:, :, 0, :], proj[:, :, ds(i * MEM_D + MQ0, MEM_D)], ACT.Square)
                        act.activation(sq[:, :, 1, :], kvm[:, :, ds(i * MEM_D, MEM_D)],
                                       ACT.Square).then_inc(M["squared"], 1)
                    if s == 2:
                        act.activation(v_head, kvm[:, :, ds(i * MEM_D + 1024, MEM_D)], ACT.Copy).then_inc(M["values"], 1)
                    if s == 4:
                        act.wait_ge(M["turned"], i + 1)
                        act.activation(qkT, at[:, 0:2, :], ACT.Copy).then_inc(M["copied"], 1)
                    if s == 6:
                        act.wait_ge(M["negmax"], i + 1)
                        for t in range(TB):
                            e = act.activation(pm[:, t, 0:256], at[:, 2, t * 256:(t + 1) * 256], ACT.Exp,
                                               bias=nmx[:, 0, t:t + 1], scale=MEM_D ** -0.5,
                                               accum_out=den[:, 0, t:t + 1])
                        e.then_inc(M["exped"], 1)
                    if s == 9:
                        act.wait_ge(M["pT_ps"], i + 1)
                        act.activation(pT[:, :, 0:256], at[:, 3, :].rearrange("p (a b) -> p a b", a=2),
                                       ACT.Copy).then_inc(M["pT"], 1)
                    if s == 11:
                        act.wait_ge(M["ov"], i + 1)
                        act.activation(oT_hi[:, ds(i * 2, 2), :], at[:, 1, :].rearrange("p (a b) -> p a b", a=2),
                                       ACT.Copy).then_inc(M["hi"], 1)
                    projections(i, s, 0)
            def diff_squares(i):
                act.activation(sq[:, :, 0, :], proj[:, :, ds(i * 256 + DA_Q0, 256)], ACT.Square)
                act.activation(sq[:, :, 1, :], proj[:, :, ds(i * 256 + DA_K0, 256)],
                               ACT.Square).then_inc(A["squared"], 1)

            for n in range(32):
                if n == 1:
                    diff_squares(0)
                projections(n // 16, n % 16, 4)

            def gate(i, s, g0, u0):
                if s == 8:
                    act.wait_ge(pair_used, i * 12 + (g0 + 8))
                    act.wait_ge(acc_free[1], i + (u0 + 1))
                    act.wait_ge(row_half, 1)
                    for t in range(TB):
                        e = act.activation(sg[:, t], acc[0][:, t, :], ACT.Tanh, scale=half_rstd[:, t:t + 1])
                    e.then_inc(acc_free[0], 1)

            def diff_attention(i, last):
                for s in range(12):
                    if s == 3:
                        act.wait_ge(A["turned"], i + 1)
                        for j in range(2):
                            e = act.activation(qkT[:, j, :], at[:, 2 * j, :], ACT.Copy)
                        e.then_inc(A["copied"], 1)
                    if s == 5:
                        act.wait_ge(A["negmax"], i + 1)
                        for b in range(4):
                            for t, (c0, c1) in enumerate(((0, 128), (128, 384))):
                                e = act.activation(pm[:, b, c0:c1], at[:, b, c0:c1], ACT.Exp,
                                                   bias=nmx[:, b, t:t + 1], scale=DA_D ** -0.5,
                                                   accum_out=den[:, b, t:t + 1])
                        e.then_inc(A["exped"], 1)
                    if s == 8:
                        act.wait_ge(A["pT_ps"], i + 1)
                        for j in range(2):
                            e = act.activation(pT[:, j, :], at[:, 2 * j, 0:384], ACT.Copy)
                        e.then_inc(A["pT"], 1)
                    gate(i, s, G_MB, U_MB)
                    if s == 9:
                        act.wait_ge(A["ov"], i + 1)
                        for j in range(2):
                            e = act.activation(sq[:, j, 0, :], at[:, 2 * j + 1, 0:256], ACT.Square)
                        e.then_inc(A["osq"], 1)
                    if s == 10 and not last:
                        act.wait_ge(A["osum"], i + 1)
                        diff_squares(i + 1)
                    if s == 11:
                        act.wait_ge(A["oT_ps"], i + 1)
                        act.activation(oT_hi[:, ds(i * 2 + 8, 2), :], at[:, 1, :].rearrange("p (a b) -> p a b", a=2),
                                       ACT.Copy).then_inc(A["hi"], 1)
                    high(i * 12 + (G_MB + s), s)

            with act.Fori(0, 3) as i:
                diff_attention(i, False)
            diff_attention(3, True)

            with act.Fori(0, 4) as i:
                for s in range(12):
                    if s == 0:
                        for j in range(2):
                            e = act.activation(dec[:, j, 0:256], rel[:], ACT.Exp, scale=sc[:, ds(i * 2 + (NROT + j), 1)])
                        e.then_inc(R["decays"], 1)
                        act.activation(tanh_g, proj[:, :, ds(i * 256 + RT_G0, 256)].rearrange(
                                           "p t (j d) -> p t j d", j=2), ACT.Tanh,
                                       scale=0.5).then_inc(R["tanh"], 1)
                    if s == 3:
                        act.wait_ge(R["turned"], i + 1)
                        act.activation(qkT[:, 0, :], at[:, 0, :], ACT.Copy).then_inc(R["copied"], 1)
                    if s == 7:
                        act.wait_ge(R["ov"], i + 1)
                        act.activation(sq[:, :, 0, :], at[:, 3, :].rearrange("p (a b) -> p a b", a=2),
                                       ACT.Square).then_inc(R["osq"], 1)
                    gate(i, s, G_DB, U_DB)
                    if s == 10:
                        act.wait_ge(R["oT_ps"], i + 1)
                        act.activation(oT_hi[:, ds(i * 2, 2), :], at[:, 0, :].rearrange("p (a b) -> p a b", a=2),
                                       ACT.Copy).then_inc(R["hi"], 1)
                    high(i * 12 + (G_DB + s), s)

            with act.Fori(0, 3) as i:
                for s in range(12):
                    gate(i, s, G_RB, U_RB)
                    high(i * 12 + (G_RB + s), s)
            for s in range(12):
                gate(3, s, G_RB, U_RB)
                if 1 <= s <= 4:
                    high_columns(2 * KD, range(2 * s - 2, 2 * s), oT_hi, lambda k: 0.5, 8)
                high(36 + G_RB + s, s)
            high_columns(2 * KD, range(8, 12), oT_hi, lambda k: 0.5, 8)

            def residual_squares(n):
                act.wait_ge(acc_free[n % 2], U_OUT + n // 2 + 2)
                act.wait_ge(row_sq, 4 + 2 * n)
                for t in range(TB):
                    act.activation(kvm[:, t, 0:NCOL], proj[:, t, n * NCOL:(n + 1) * NCOL], ACT.Square,
                                   accum_out=x2_ss[:, t, n:n + 1]).then_inc(row_sq, 1)

            def residual_columns(n):
                high_columns(3 * KD, range(4 * n, 4 * n + 4), hT_hi, lambda k: g_cols[:, 2 * KD + k:2 * KD + k + 1])

            for s in range(32):
                if s == 2:
                    high_columns(2 * KD, range(12, KD), oT_hi, lambda k: 0.5, 8)
                if s >= 8 and s % 8 == 1:
                    residual_squares(s // 8 - 1)
                if s >= 8 and s % 8 == 2:
                    residual_columns(s // 8 - 1)
                high(G_OUT + s, s)
            residual_squares(3)

            def silu(g, u, f):
                act.wait_ge(pair_used, g + 1)
                if f is not None:
                    act.wait_ge(acc_free[1], u + 1)
                for t in range(TB):
                    e = act.activation(sg[:, t], acc[0][:, t, :], ACT.Silu, scale=row_rstd[:, 2, t:t + 1])
                e.then_inc(acc_free[0], 1)

            def high_acts(f, dst):
                act.wait_ge(ff_ps, f)
                act.activation(dst[:, 0:4, :], at[:, 0:2, :].rearrange("p b (a c) -> p (b a) c", a=2),
                               ACT.Copy).then_inc(ff_hi, 1)

            for s in range(16):
                if s == 2:
                    residual_columns(3)
                if s == 8:
                    act.wait_ge(row_root, 6)
                    silu(G_F0 + 7, U_F0, None)
                high(G_F0 + s, s)
            def feed_forward(f, s):
                if s == 3:
                    high_acts(f, oT_hi)
                if s == 8:
                    silu(f * 24 + (G_F - 24 + 7), f * 3 + (U_F - 3), f)
                high(f * 24 + (G_F - 24 + s), s)

            with act.Fori(1, NF - 1) as f:
                for s in range(24):
                    feed_forward(f, s)
            for s in range(24):
                if s == 19:
                    high_acts(NF, hT_hi)
                feed_forward(NF - 1, s)
            for s in range(4):
                high(G_END + s, s)

        @block.vector
        def _(v):
            def step(ins, s, value):
                ins.then_inc(s, 1)
                v.wait_ge(s, value)

            def low(g, s):
                v.wait_ge(hi_done, g + (RING + 1))
                v.tensor_tensor(w_lo[:, s % RING], raw[:, s % RING], w_hi[:, s % RING].bitcast(F32),
                                ALU.subtract).then_inc(lo_done, 1)

            def row_means(k):
                for t in range(TB):
                    v.wait_ge(row_sq, 2 * k + t + 1)
                    v.tensor_scalar(row_ms[:, k, t:t + 1], row_ss[:, k, t:t + 1], 1.0 / D, EPS, ALU.mult,
                                    ALU.add).then_inc(row_mean, 1)

            def low_columns(n0, ks, dst, hi, scale, shift=0):
                for k in ks:
                    v.wait_ge(col_hi, n0 + k + 1)
                    v.scalar_tensor_tensor(out=dst[:, (k + shift) % KD, :], in0=at[:, k % 4, 0:TOK], scalar=scale(k),
                                           in1=hi[:, (k + shift) % KD, :].bitcast(F32), op0=ALU.mult,
                                           op1=ALU.subtract).then_inc(col_lo, 1)

            def mean_squares(src, n, width, i, X, summed, mean):
                step(v.tensor_reduce(ss[:, 0:n], src, AX.X, ALU.add), X[summed], i + 1)
                v.tensor_scalar(ms[:, 0:n], ss[:, 0:n], 1.0 / width, EPS, ALU.mult, ALU.add).then_inc(X[mean], 1)

            for p in range(2):
                v.nop().then_inc(acc_free[p], 1)
            v.wait_ge(gcol_ps, 1)
            step(v.tensor_copy(g_cols[:], at[:, 3, 0:3 * KD]), gcol_ok, 1)
            low_columns(0, range(2), oT_lo, oT_hi, lambda k: g_cols[:, k:k + 1])
            for s in range(RING):
                v.wait_ge(hi_done, s + 1)
                v.tensor_tensor(w_lo[:, s], raw[:, s], w_hi[:, s].bitcast(F32), ALU.subtract).then_inc(lo_done, 1)
                low_columns(0, range(2 + 2 * s, 4 + 2 * s), oT_lo, oT_hi, lambda k: g_cols[:, k:k + 1])
            low_columns(0, range(10, KD), oT_lo, oT_hi, lambda k: g_cols[:, k:k + 1])
            for s in range(16):
                if s == 3:
                    row_means(0)
                if s == 6:
                    row_means(1)
                if s >= 8:
                    low_columns(KD, range(2 * s - 16, 2 * s - 14), hT_lo, hT_hi,
                                lambda k: g_cols[:, KD + k:KD + k + 1])
                low(G_KV + s, s)
            with v.Fori(1, 2) as i:
                for s in range(16):
                    low(i * 16 + (G_KV + s), s)

            def angles():
                v.wait_ge(const_in, 16 * 12)
                step(v.tensor_copy(pos_f[:], pos_i[:]), setup_v, 1)
                for t in range(TB):
                    for k in range(2):
                        e = v.tensor_scalar(ang[:, k, t, :], sc[:, 0:NROT], pos_f[:, t:t + 1], None, ALU.mult)
                step(e, setup_v, 2)
                for k in range(2):
                    e = v.tensor_scalar(turns[:, k], ang[:, k], 1.0 / (2.0 * np.pi), 0.25 * k, ALU.mult, ALU.add)
                step(e, setup_v, 3)
                step(v.tensor_scalar(turns, turns, ROUND, None, ALU.add), setup_v, 4)
                step(v.tensor_scalar(turns, turns, -ROUND, None, ALU.add), setup_v, 5)
                for n, part in enumerate(TWO_PI):
                    step(v.scalar_tensor_tensor(out=ang, in0=turns, scalar=-part, in1=ang, op0=ALU.mult,
                                                op1=ALU.add), setup_v, 6 + n)
                v.tensor_tensor(lam_pr, lam_in[:, 0], lam_in[:, 1], ALU.mult)
                step(v.tensor_scalar(ang[:, 1], ang[:, 1], 0.5 * np.pi, None, ALU.add), setup_v, 9)
                step(v.tensor_scalar(ang, ang, 3.1415925, -3.1415925, ALU.min, ALU.max), setup_v, 10)
                v.tensor_reduce(lam_s[:], lam_pr[:], AX.X, ALU.add).then_inc(setup_v, 1)

            def rotary_and_lambda():
                v.wait_ge(setup_a, 2)
                step(v.tensor_tensor(neg_lam[:], lam_e[:, 1:2], lam_e[:, 0:1], ALU.subtract), setup_v, 12)
                v.tensor_scalar(neg_lam[:], neg_lam[:], -LAMBDA_INIT, None, ALU.add)
                v.tensor_scalar(g_sub[:], g_sub[:], 1.0 - LAMBDA_INIT, None, ALU.mult)
                step(v.tensor_scalar(g_ret[:], g_ret[:], 0.5, None, ALU.mult), setup_v, 13)
                v.wait_ge(row_root, 4)
                v.tensor_scalar(half_rstd[:], row_rstd[:, 1, :], 0.5, None, ALU.mult).then_inc(row_half, 1)

            for s in range(16):
                if s == 2:
                    angles()
                if s == 6:
                    rotary_and_lambda()
                low(G_MQ + s, s)

            with v.Fori(0, MEM_H) as i:
                for s in range(16):
                    if s == 0:
                        v.wait_ge(M["squared"], i + 1)
                        mean_squares(sq[:].rearrange("p t k d -> p (t k) d"), 4, MEM_D, i, M, "summed", "mean")
                        v.wait_ge(M["root"], i + 1)
                        for t in range(TB):
                            for k, src in enumerate((proj[:, t, ds(i * MEM_D + MQ0, MEM_D)],
                                                     kvm[:, t, ds(i * MEM_D, MEM_D)])):
                                e = v.scalar_tensor_tensor(out=qn[:, t, k, :], in0=src,
                                                           scalar=rstd[:, 2 * t + k:2 * t + k + 1],
                                                           in1=g_mem[:, k, :], op0=ALU.mult, op1=ALU.mult)
                        e.then_inc(M["normed"], 1)
                    if s == 6:
                        v.wait_ge(M["scored"], i + 1)
                        step(v.tensor_reduce(mx[:, 0, :], at[:, 2, :].rearrange("p (t k) -> p t k", t=2), AX.X,
                                             ALU.max), M["maxed"], i + 1)
                        v.tensor_scalar(nmx[:, 0, :], mx[:, 0, :], -MEM_D ** -0.5, None,
                                        ALU.mult).then_inc(M["negmax"], 1)
                    if s == 7:
                        v.wait_ge(M["exped"], i + 1)
                        step(v.reciprocal(rden[:, 0, :], den[:, 0, :]), M["recip"], i + 1)
                        for t in range(TB):
                            e = v.tensor_scalar(pm[:, t, 0:256], pm[:, t, 0:256], rden[:, 0, t:t + 1], None, ALU.mult)
                        e.then_inc(M["weighed"], 1)
                    if s == 11:
                        v.wait_ge(M["hi"], i + 1)
                        v.tensor_tensor(oT_lo[:, ds(i * 2, 2), :], at[:, 1, :].rearrange("p (a b) -> p a b", a=2),
                                        oT_hi[:, ds(i * 2, 2), :].bitcast(F32), ALU.subtract).then_inc(M["lo"], 1)
                    low(i * 16 + (G_PROJ + s), s)
            def diff_means(i):
                v.wait_ge(A["squared"], i + 1)
                mean_squares(sq[:].rearrange("p t k (m d) -> p (t k m) d", d=DA_D), 16, DA_D, i, A,
                             "summed", "mean")

            def diff_normalise(i):
                v.wait_ge(A["root"], i + 1)
                r = rstd[:].rearrange("p (t k m) -> p t k m", t=2, k=2)
                for k, c0 in enumerate((DA_Q0, DA_K0)):
                    e = v.tensor_tensor(qn[:, :, k, :].rearrange("p t (m d) -> p t m d", d=DA_D),
                                        proj[:, :, ds(i * 256 + c0, 256)].rearrange("p t (m d) -> p t m d", d=DA_D),
                                        r[:, :, k, :].unsqueeze(3).to_broadcast([P, 2, 4, DA_D]), ALU.mult)
                step(e, A["scaled"], i + 1)
                for k in range(2):
                    q = qn[:, :, k, :].rearrange("p t (m d) -> p t m d", d=DA_D)
                    e = v.tensor_tensor(q, q, g_da[:, k, :].unsqueeze(1).unsqueeze(1).to_broadcast([P, 2, 4, DA_D]),
                                        ALU.mult)
                step(e, A["gained"], i + 1)

            def diff_rotate(i):
                q = qn[:].rearrange("p t k (m d) -> p t (k m) d", d=DA_D)
                sin = trig[:, 0, :, 0:R1].unsqueeze(2).to_broadcast([P, 2, 8, R1])
                cos = trig[:, 1, :, 0:R1].unsqueeze(2).to_broadcast([P, 2, 8, R1])
                tv = tmp2.rearrange("p n (t m d) -> p n t m d", t=2, m=8)
                x1, x2 = q[:, :, :, 0:R1], q[:, :, :, R1:2 * R1]
                v.tensor_tensor(tv[:, 0], x1, cos, ALU.mult)
                v.tensor_tensor(tv[:, 1], x2, sin, ALU.mult)
                v.tensor_tensor(tv[:, 2], x2, cos, ALU.mult)
                step(v.tensor_tensor(tv[:, 3], x1, sin, ALU.mult), A["rprod"], i + 1)
                v.tensor_tensor(x1, tv[:, 0], tv[:, 1], ALU.subtract)
                v.tensor_tensor(x2, tv[:, 2], tv[:, 3], ALU.add).then_inc(A["rot"], 1)

            for n in range(32):
                if n == 2:
                    diff_means(0)
                if n == 4:
                    diff_normalise(0)
                if n == 5:
                    diff_rotate(0)
                low(G_PROJ + 64 + n, n)

            def gated(i, s, g0, u0, first, n0):
                if s == 11:
                    v.wait_ge(pair_used, i * 12 + (g0 + 12))
                    v.wait_ge(acc_free[0], i + (u0 + 2))
                    dst = kvm[:, :, ds(i * NCOL, NCOL)]
                    e = v.scalar_tensor_tensor(out=dst if first else gt, in0=sg, scalar=1.0, in1=acc[1][:],
                                               op0=ALU.add, op1=ALU.mult)
                    e.then_inc(acc_free[1], 1)
                    if not first:
                        v.wait_ge(acc_free[1], i + (u0 + 2))
                        v.tensor_tensor(dst, dst, gt, ALU.add).then_inc(merged, 1)
                        v.wait_ge(merged, i + (n0 + 1))

            def diff_attention(i, last):
                for s in range(12):
                    if s == 4:
                        v.wait_ge(A["scored"], i + 1)
                        sd = at[:].rearrange("p b (h c) -> p b h c", h=2)[:, :, :, 0:P]
                        step(v.tensor_tensor(sd, sd, mask[:].unsqueeze(1).unsqueeze(1).to_broadcast([P, 4, 2, P]),
                                             ALU.add), A["masked"], i + 1)
                        v.tensor_reduce(mx[:, :, 0:1], at[:, :, 0:128], AX.X, ALU.max)
                        step(v.tensor_reduce(mx[:, :, 1:2], at[:, :, 128:384], AX.X, ALU.max), A["maxed"], i + 1)
                        v.tensor_scalar(nmx[:], mx[:], -DA_D ** -0.5, None, ALU.mult).then_inc(A["negmax"], 1)
                    if s == 5:
                        v.wait_ge(A["exped"], i + 1)
                        step(v.reciprocal(rden[:], den[:]), A["recip"], i + 1)
                        step(v.tensor_scalar(lrden[:], rden[:].rearrange("p (j m) t -> p j m t", m=2)[:, :, 1, :],
                                             neg_lam[:, 0:1], None, ALU.mult), A["lrecip"], i + 1)
                        spans = ((0, 128), (128, 384))
                        for j in range(2):
                            for t, (c0, c1) in enumerate(spans):
                                e = v.tensor_scalar(pm[:, 2 * j + 1, c0:c1], pm[:, 2 * j + 1, c0:c1],
                                                    lrden[:, j, t:t + 1], None, ALU.mult)
                        step(e, A["second"], i + 1)
                        for j in range(2):
                            for t, (c0, c1) in enumerate(spans):
                                e = v.scalar_tensor_tensor(out=pm[:, 2 * j, c0:c1], in0=pm[:, 2 * j, c0:c1],
                                                           scalar=rden[:, 2 * j, t:t + 1], in1=pm[:, 2 * j + 1, c0:c1],
                                                           op0=ALU.mult, op1=ALU.add)
                        e.then_inc(A["mixed"], 1)
                    if s == 9:
                        v.wait_ge(A["osq"], i + 1)
                        mean_squares(sq[:, :, 0, :].rearrange("p j (t d) -> p j t d", t=2), 4, DA_V, i, A,
                                     "osum", "omean")
                        v.wait_ge(A["oroot"], i + 1)
                        for j in range(2):
                            for t in range(TB):
                                n = 2 * j + t
                                e = v.scalar_tensor_tensor(out=osb[:, j, t * P:(t + 1) * P],
                                                           in0=at[:, 2 * j + 1, t * P:(t + 1) * P],
                                                           scalar=rstd[:, n:n + 1], in1=g_sub[:], op0=ALU.mult,
                                                           op1=ALU.mult)
                        e.then_inc(A["onorm"], 1)
                    if s == 10 and not last:
                        diff_means(i + 1)
                    if s == 11 and not last:
                        diff_normalise(i + 1)
                        diff_rotate(i + 1)
                    if s == 11:
                        v.wait_ge(A["hi"], i + 1)
                        v.tensor_tensor(oT_lo[:, ds(i * 2 + 8, 2), :], at[:, 1, :].rearrange("p (a b) -> p a b", a=2),
                                        oT_hi[:, ds(i * 2 + 8, 2), :].bitcast(F32), ALU.subtract).then_inc(A["lo"], 1)
                    gated(i, s, G_MB, U_MB, True, 0)
                    low(i * 12 + (G_MB + s), s)

            with v.Fori(0, 3) as i:
                diff_attention(i, False)
            diff_attention(3, True)

            with v.Fori(0, 4) as i:
                for s in range(12):
                    if s == 0:
                        H = RT_D // 2
                        for t in range(TB):
                            qk = proj[:, t, RT_Q0:RT_V0].rearrange("p (k c) -> p k c", k=2)[:, :, ds(i * 128, 128)]
                            qk = qk.rearrange("p k (j d) -> p k j d", j=2)
                            x1, x2 = qk[:, :, :, 0:H], qk[:, :, :, H:2 * H]
                            sin = trig[:, 0, t, R1:NROT].unsqueeze(1).unsqueeze(1).to_broadcast([P, 2, 2, H])
                            cos = trig[:, 1, t, R1:NROT].unsqueeze(1).unsqueeze(1).to_broadcast([P, 2, 2, H])
                            tv = tmp.rearrange("p n (k j d) -> p n k j d", k=2, j=2)
                            dst = qn[:, t, :, 0:128].rearrange("p k (j d) -> p k j d", j=2)
                            v.tensor_tensor(tv[:, 0], x1, cos, ALU.mult)
                            v.tensor_tensor(tv[:, 1], x2, sin, ALU.mult)
                            v.tensor_tensor(tv[:, 2], x2, cos, ALU.mult)
                            step(v.tensor_tensor(tv[:, 3], x1, sin, ALU.mult), R["rprod"], i * 2 + (t + 1))
                            v.tensor_tensor(dst[:, :, :, 0:H], tv[:, 0], tv[:, 1], ALU.subtract)
                            step(v.tensor_tensor(dst[:, :, :, H:2 * H], tv[:, 2], tv[:, 3], ALU.add), R["rot"],
                                 i * 2 + (t + 1))
                    if s == 5:
                        v.wait_ge(R["scored"], i + 1)
                        v.wait_ge(R["decays"], i + 1)
                        for j in range(2):
                            for c0, c1 in ((0, 256), (256, 384)):
                                e = v.scalar_tensor_tensor(out=pm[:, j, c0:c1], in0=at[:, 1 + j, c0:c1],
                                                           scalar=RT_D ** -0.5, in1=dec[:, j, 0:c1 - c0],
                                                           op0=ALU.mult, op1=ALU.mult)
                        e.then_inc(R["weighed"], 1)
                    if s == 7:
                        v.wait_ge(R["tanh"], i + 1)
                        for t in range(TB):
                            e = v.scalar_tensor_tensor(out=tanh_g[:, t], in0=tanh_g[:, t], scalar=1.0,
                                               in1=proj[:, t, ds(i * 256 + RT_G0, 256)].rearrange(
                                                   "p (j d) -> p j d", j=2), op0=ALU.add,
                                               op1=ALU.mult)
                        e.then_inc(R["gmul"], 1)
                        v.wait_ge(R["osq"], i + 1)
                        mean_squares(sq[:, :, 0, :].rearrange("p t (j d) -> p t j d", j=2), 4, RT_V, i, R,
                                     "osum", "omean")
                        v.wait_ge(R["oroot"], i + 1)
                        for n in range(4):
                            e = v.scalar_tensor_tensor(out=osb[:, n // 2, (n % 2) * P:(n % 2 + 1) * P],
                                                       in0=at[:, 3, n * P:(n + 1) * P], scalar=rstd[:, n:n + 1],
                                                       in1=g_ret[:], op0=ALU.mult, op1=ALU.mult)
                        step(e, R["onorm"], i + 1)
                        v.wait_ge(R["gmul"], i + 1)
                        o4 = osb.rearrange("p t (j d) -> p t j d", j=2)
                        v.tensor_tensor(o4, o4, tanh_g, ALU.mult).then_inc(R["gated"], 1)
                    if s == 10:
                        v.wait_ge(R["hi"], i + 1)
                        v.tensor_tensor(oT_lo[:, ds(i * 2, 2), :], at[:, 0, :].rearrange("p (a b) -> p a b", a=2),
                                        oT_hi[:, ds(i * 2, 2), :].bitcast(F32), ALU.subtract).then_inc(R["lo"], 1)
                    gated(i, s, G_DB, U_DB, False, 0)
                    low(i * 12 + (G_DB + s), s)

            with v.Fori(0, 3) as i:
                for s in range(12):
                    gated(i, s, G_RB, U_RB, False, 4)
                    low(i * 12 + (G_RB + s), s)
            for s in range(12):
                gated(3, s, G_RB, U_RB, False, 4)
                if 1 <= s <= 4:
                    low_columns(2 * KD, range(2 * s - 2, 2 * s), oT_lo, oT_hi, lambda k: 0.5, 8)
                low(36 + G_RB + s, s)
            low_columns(2 * KD, range(8, 12), oT_lo, oT_hi, lambda k: 0.5, 8)

            def residual(g, p, dst):
                v.wait_ge(pair_used, g + 1)
                v.tensor_tensor(dst, acc[p][:], dst, ALU.add).then_inc(acc_free[p], 1)

            v.wait_ge(x_again, 32)
            def residual_columns(n):
                low_columns(3 * KD, range(4 * n, 4 * n + 4), hT_lo, hT_hi,
                            lambda k: g_cols[:, 2 * KD + k:2 * KD + k + 1])

            for s in range(32):
                if s == 2:
                    low_columns(2 * KD, range(12, KD), oT_lo, oT_hi, lambda k: 0.5, 8)
                if s >= 8 and s % 8 == 2:
                    residual_columns(s // 8 - 1)
                if s % 8 == 7:
                    n = s // 8
                    residual(G_OUT + s, n % 2, proj[:, :, n * NCOL:(n + 1) * NCOL])
                low(G_OUT + s, s)

            def activations(g, u, f):
                v.wait_ge(pair_used, g + 1)
                v.wait_ge(acc_free[0], u + 2)
                if f is not None:
                    v.wait_ge(ff_ps, f)
                for t in range(TB):
                    e = v.scalar_tensor_tensor(out=gt[:, t], in0=acc[1][:, t, :], scalar=row_rstd[:, 2, t:t + 1],
                                               in1=sg[:, t], op0=ALU.mult, op1=ALU.mult)
                e.then_inc(acc_free[1], 1)

            def low_acts(f, dst, hi):
                v.wait_ge(ff_hi, f)
                v.tensor_tensor(dst[:, 0:4, :], at[:, 0:2, :].rearrange("p b (a c) -> p (b a) c", a=2),
                                hi[:, 0:4, :].bitcast(F32), ALU.subtract).then_inc(ff_lo, 1)

            for s in range(16):
                if s == 2:
                    residual_columns(3)
                if s == 3:
                    v.wait_ge(row_sq, 4 + 8)
                    step(v.tensor_reduce(row_ss[:, 2, :], x2_ss[:], AX.X, ALU.add), row_sum, 1)
                    v.tensor_scalar(row_ms[:, 2, :], row_ss[:, 2, :], 1.0 / D, EPS, ALU.mult,
                                    ALU.add).then_inc(row_mean, 1)
                if s == 15:
                    v.wait_ge(row_root, 6)
                    activations(G_F0 + s, U_F0, None)
                low(G_F0 + s, s)
            def feed_forward(f, s):
                if s == 3:
                    low_acts(f, oT_lo, oT_hi)
                if s == 15:
                    activations(f * 24 + (G_F - 24 + s), f * 3 + (U_F - 3), f)
                if s in (17, 19, 21, 23):
                    n = (s - 17) // 2
                    residual(f * 24 + (G_F - 24 + s), n % 2, proj[:, :, n * NCOL:(n + 1) * NCOL])
                low(f * 24 + (G_F - 24 + s), s)

            with v.Fori(1, NF - 1) as f:
                for s in range(24):
                    feed_forward(f, s)
            for s in range(24):
                if s == 19:
                    low_acts(NF, hT_lo, hT_hi)
                feed_forward(NF - 1, s)
            for s in range(8):
                if s == 7:
                    for t in range(TB):
                        v.wait_ge(end_done, t + 1)
                        v.tensor_tensor(proj[:, t, D - NCOL:D], acc[1][:, t, :], proj[:, t, D - NCOL:D],
                                        ALU.add).then_inc(end_added, 1)
                elif s % 2 == 1:
                    n = s // 2
                    residual(G_END + s, n % 2, proj[:, :, n * NCOL:(n + 1) * NCOL])
                if s < 4:
                    low(G_END + s, s)

        @block.tensor
        def _(pe):
            def three_passes(s, hi, lo, k0, p, k, t, first, last):
                tok = slice(t * P, (t + 1) * P)
                for n, (a, w) in enumerate(((hi, w_hi), (hi, w_lo), (lo, w_hi))):
                    e = pe.matmul(acc[p][:, t, :], a[:, k0 + k, tok], w[:, s % RING, k, :],
                                  start=first and k == 0 and n == 0, stop=last and k == 1 and n == 2)
                return e

            def pair(g, s, hi, lo, k0, p, first, last, col=None):
                pe.wait_ge(lo_done, g + 1)
                if col is not None:
                    pe.wait_ge(col_lo, col)
                for k in range(2):
                    for t in range(TB):
                        e = three_passes(s, hi, lo, k0, p, k, t, first, last)
                return e

            def chunk_pair(g, s, hi, lo, k0, kk, nk, u, p, col=None):
                if kk == 0:
                    pe.wait_ge(acc_free[p], u + 1)
                e = pair(g, s, hi, lo, k0 + 2 * kk, p, kk == 0, kk == nk - 1, col)
                e.then_inc(pair_used, 1)

            def turn(out, src):
                return pe.transpose(out, src, ident[:])

            def turn_columns(n0, ks, src, c0):
                for k in ks:
                    if n0 + k >= 4:
                        pe.wait_ge(col_lo, n0 + k - 3)
                    for t in range(TB):
                        e = turn(at[:, k % 4, t * P:(t + 1) * P], src[:, t, c0 + k * P:c0 + (k + 1) * P])
                    e.then_inc(col_ps, 1)

            pe.wait_ge(rows_in, 16 * 3)
            pe.wait_ge(masks, 3)
            pe.transpose(at[:, 3, 0:3 * KD], g_rows, ident[0:3 * KD, 0:3 * KD]).then_inc(gcol_ps, 1)
            pe.wait_ge(gcol_ok, 1)
            pe.wait_ge(mem_in[0], 16)
            turn_columns(0, range(4), proj, 0)
            for s in range(16):
                if s in (0, 1, 2):
                    pe.wait_ge(mem_in[s + 1], 16)
                    turn_columns(0, range(4 * s + 4, 4 * s + 8), proj, 0)
                chunk_pair(G_KV + s, s, oT_hi, oT_lo, 0, s % 8, 8, U_KV, s // 8, 2 * s + 2 if s < 8 else None)
                if s == 7:
                    for t in range(TB):
                        pe.wait_ge(x_in[t], 16)
                if s >= 7 and s < 15:
                    turn_columns(KD, range(2 * s - 14, 2 * s - 12), proj, D)
            with pe.Fori(1, 2) as i:
                for s in range(16):
                    chunk_pair(i * 16 + (G_KV + s), s, oT_hi, oT_lo, 0, s % 8, 8, i + U_KV, s // 8)
            pe.wait_ge(col_lo, 2 * KD)
            for s in range(16):
                chunk_pair(G_MQ + s, s, hT_hi, hT_lo, 0, s % 8, 8, U_MQ, s // 8)

            with pe.Fori(0, MEM_H) as i:
                for s in range(16):
                    chunk_pair(i * 16 + (G_PROJ + s), s, hT_hi, hT_lo, 0, s % 8, 8, i + U_PROJ, s // 8)
                    if s == 3:
                        pe.wait_ge(M["normed"], i + 1)
                        for k in range(2):
                            for h in range(2):
                                for t in range(TB):
                                    e = turn(at[:, k, h * 256 + t * P:h * 256 + (t + 1) * P],
                                             qn[:, t, k, h * P:(h + 1) * P])
                        e.then_inc(M["turned"], 1)
                    if s == 5:
                        pe.wait_ge(M["copied"], i + 1)
                        for t in range(TB):
                            for h in range(2):
                                e = pe.matmul(at[:, 2, t * 256:(t + 1) * 256],
                                              qkT[:, 0, h * 256 + t * P:h * 256 + (t + 1) * P],
                                              qkT[:, 1, h * 256:(h + 1) * 256], start=h == 0, stop=h == 1)
                        e.then_inc(M["scored"], 1)
                    if s == 8:
                        pe.wait_ge(M["weighed"], i + 1)
                        for k in range(2):
                            for t in range(TB):
                                e = turn(at[:, 3, k * 256 + t * P:k * 256 + (t + 1) * P], pm[:, t, k * P:(k + 1) * P])
                        e.then_inc(M["pT_ps"], 1)
                    if s == 10:
                        pe.wait_ge(M["values"], i + 1)
                        pe.wait_ge(M["pT"], i + 1)
                        for h in range(2):
                            for k in range(2):
                                e = pe.matmul(at[:, 1, h * 256:(h + 1) * 256],
                                              v_head[:, k, h * P:(h + 1) * P], pT[:, k, 0:256],
                                              start=k == 0, stop=k == 1)
                        e.then_inc(M["ov"], 1)
            with pe.Fori(0, 2) as i:
                for s in range(16):
                    chunk_pair(i * 16 + (G_PROJ + 64 + s), s, hT_hi, hT_lo, 0, s % 8, 8, i + (U_PROJ + 4), s // 8)

            def gate_branch(i, s, g0, u0, k0, outputs, count):
                if s == 8:
                    pe.wait_ge(outputs, count)
                if s < 8:
                    chunk_pair(i * 12 + (g0 + s), s, hT_hi, hT_lo, 0, s, 8, i + u0, 0)
                else:
                    chunk_pair(i * 12 + (g0 + s), s, oT_hi, oT_lo, k0, s - 8, 4, i + u0, 1)

            with pe.Fori(0, 4) as i:
                for s in range(12):
                    gate_branch(i, s, G_MB, U_MB, 0, M["lo"], MEM_H)
                    if s == 2:
                        pe.wait_ge(A["rot"], i + 1)
                        for j in range(2):
                            for k in range(2):
                                for t in range(TB):
                                    e = turn(at[:, 2 * j, k * 256 + t * P:k * 256 + (t + 1) * P],
                                             qn[:, t, k, j * P:(j + 1) * P])
                        e.then_inc(A["turned"], 1)
                    if s == 3:
                        pe.wait_ge(A["copied"], i + 1)
                        for j in range(2):
                            for m in range(2):
                                row = slice(m * DA_D, (m + 1) * DA_D)
                                pe.matmul(at[:, 2 * j + m, 0:128], qkT[row, j, 0:128], qkT[row, j, 256:384],
                                          start=True, stop=True)
                                e = pe.matmul(at[:, 2 * j + m, 128:384], qkT[row, j, 128:256],
                                              qkT[row, j, 256:512], start=True, stop=True)
                        e.then_inc(A["scored"], 1)
                    if s == 7:
                        pe.wait_ge(A["mixed"], i + 1)
                        for j in range(2):
                            for n in range(3):
                                e = turn(at[:, 2 * j, n * P:(n + 1) * P], pm[:, 2 * j, n * P:(n + 1) * P])
                        e.then_inc(A["pT_ps"], 1)
                    if s == 8:
                        pe.wait_ge(A["pT"], i + 1)
                        for j in range(2):
                            v0 = proj[:, 0, ds(i * 256 + (DA_V0 + j * P), P)]
                            v1 = proj[:, 1, ds(i * 256 + (DA_V0 + j * P), P)]
                            pe.matmul(at[:, 2 * j + 1, 0:128], pT[:, j, 0:128], v0, start=True, stop=True)
                            pe.matmul(at[:, 2 * j + 1, 128:256], pT[:, j, 128:256], v0, start=True, stop=False)
                            e = pe.matmul(at[:, 2 * j + 1, 128:256], pT[:, j, 256:384], v1, start=False, stop=True)
                        e.then_inc(A["ov"], 1)
                    if s == 11:
                        pe.wait_ge(A["onorm"], i + 1)
                        for j in range(2):
                            for t in range(TB):
                                e = turn(at[:, 1, j * 256 + t * P:j * 256 + (t + 1) * P], osb[:, j, t * P:(t + 1) * P])
                        e.then_inc(A["oT_ps"], 1)

            with pe.Fori(0, 4) as i:
                for s in range(12):
                    gate_branch(i, s, G_DB, U_DB, 8, A["lo"], 4)
                    if s == 2:
                        pe.wait_ge(R["rot"], i * 2 + 2)
                        for k in range(2):
                            for t in range(TB):
                                e = turn(at[:, 0, k * 256 + t * P:k * 256 + (t + 1) * P], qn[:, t, k, 0:128])
                        e.then_inc(R["turned"], 1)
                    if s == 4:
                        pe.wait_ge(R["copied"], i + 1)
                        for j in range(2):
                            row = slice(j * RT_D, (j + 1) * RT_D)
                            pe.matmul(at[:, 1 + j, 0:256], qkT[row, 0, 256:384], qkT[row, 0, 0:256],
                                      start=True, stop=True)
                            e = pe.matmul(at[:, 1 + j, 256:384], qkT[row, 0, 384:512], qkT[row, 0, 128:256],
                                          start=True, stop=True)
                        e.then_inc(R["scored"], 1)
                    if s == 6:
                        pe.wait_ge(R["weighed"], i + 1)
                        for j in range(2):
                            v0 = proj[:, 0, ds(i * 256 + (RT_V0 + j * P), P)]
                            v1 = proj[:, 1, ds(i * 256 + (RT_V0 + j * P), P)]
                            o0, o1 = at[:, 3, j * P:(j + 1) * P], at[:, 3, 256 + j * P:256 + (j + 1) * P]
                            pe.matmul(o0, pm[:, j, 0:128], v0, start=True, stop=True)
                            pe.matmul(o1, pm[:, j, 128:256], v0, start=True, stop=False)
                            e = pe.matmul(o1, pm[:, j, 256:384], v1, start=False, stop=True)
                        e.then_inc(R["ov"], 1)
                    if s == 9:
                        pe.wait_ge(R["gated"], i + 1)
                        for j in range(2):
                            for t in range(TB):
                                e = turn(at[:, 0, j * 256 + t * P:j * 256 + (t + 1) * P], osb[:, t, j * P:(j + 1) * P])
                        e.then_inc(R["oT_ps"], 1)

            with pe.Fori(0, 3) as i:
                for s in range(12):
                    gate_branch(i, s, G_RB, U_RB, 0, R["lo"], 4)
            for s in range(12):
                gate_branch(3, s, G_RB, U_RB, 0, R["lo"], 4)
                if s == 0:
                    pe.wait_ge(merged, 7)
                if s < 4:
                    turn_columns(2 * KD, range(2 * s, 2 * s + 2), kvm, 0)
            turn_columns(2 * KD, range(8, 12), kvm, 0)
            for s in range(32):
                chunk_pair(G_OUT + s, s, oT_hi, oT_lo, 8 - 16 * (s % 8 > 3), s % 8, 8, U_OUT + s // 16, (s // 8) % 2,
                           2 * KD + 2 * s + 2 if s < 8 else None)
                if s == 1:
                    pe.wait_ge(merged, 8)
                    turn_columns(2 * KD, range(12, KD), kvm, 0)
                if s >= 8 and s % 8 == 0:
                    n = s // 8 - 1
                    pe.wait_ge(acc_free[n % 2], U_OUT + n // 2 + 2)
                    turn_columns(3 * KD, range(4 * n, 4 * n + 4), proj, 0)

            def turn_acts(drained):
                pe.wait_ge(acc_free[1], drained)
                for k in range(4):
                    for t in range(TB):
                        c0 = (k % 2) * 256 + t * P
                        e = turn(at[:, k // 2, c0:c0 + P], gt[:, t, k * P:(k + 1) * P])
                e.then_inc(ff_ps, 1)

            for s in range(16):
                chunk_pair(G_F0 + s, s, hT_hi, hT_lo, 0, s % 8, 8, U_F0, s // 8, 3 * KD + 2 * s + 2 if s < 8 else None)
                if s == 1:
                    pe.wait_ge(acc_free[1], U_F0 + 1)
                    turn_columns(3 * KD, range(12, KD), proj, 0)
            def feed_forward(f, s):
                g, u = f * 24 + (G_F - 24 + s), f * 3 + (U_F - 3)
                if s < 16:
                    chunk_pair(g, s, hT_hi, hT_lo, 0, s % 8, 8, u, s // 8)
                else:
                    if s == 16:
                        pe.wait_ge(ff_lo, f)
                    n = (s - 16) // 2
                    chunk_pair(g, s, oT_hi, oT_lo, 0, s % 2, 2, u + (1 + n // 2), n % 2)
                if s == 2:
                    turn_acts(f * 3 + (U_F - 2))

            with pe.Fori(1, NF - 1) as f:
                for s in range(24):
                    feed_forward(f, s)
            for s in range(24):
                feed_forward(NF - 1, s)
                if s == 17:
                    turn_acts(U_END - 1)
            pe.wait_ge(ff_lo, NF)
            for s in range(7):
                chunk_pair(G_END + s, s, hT_hi, hT_lo, 0, s % 2, 2, U_END + s // 4, (s // 2) % 2)
            pe.wait_ge(lo_done, G_END + 8)
            for t in range(TB):
                for k in range(2):
                    e = three_passes(7, hT_hi, hT_lo, 2, 1, k, t, False, True)
                e.then_inc(end_done, 1)


_INS = ['x', 'mem', 'positions', 'attn_norm_g', 'w_in', 'da_q_norm_g', 'da_k_norm_g', 'da_lambda_q1', 'da_lambda_k1',
        'da_lambda_q2', 'da_lambda_k2', 'da_subln_g', 'ret_norm_g', 'mem_norm_g', 'w_mem_kv', 'mem_q_norm_g',
        'mem_k_norm_g', 'w_o_da', 'w_o_ret', 'w_o_mem', 'w_out', 'ffn_norm_g', 'w_ffn_gate', 'w_ffn_up', 'w_ffn_down']


def kernel(**inputs):
    import concourse.bacc as _bacc
    from concourse.bass_utils import run_bass_kernel_spmd as _run

    nc = _bacc.Bacc("TRN2", target_bir_lowering=False, num_devices=1)
    arrays, args = {}, []
    for name in _INS + ["shape_consts"]:
        a = shape_constants() if name == "shape_consts" else np.ascontiguousarray(inputs[name])
        arrays[f"in_{name}"] = a
        args.append(nc.dram_tensor(f"in_{name}", a.shape, mybir.dt.from_np(a.dtype), kind="ExternalInput").ap())
    args.append(nc.dram_tensor("out_0", (1, TOK, D), F32, kind="ExternalOutput").ap())
    program(nc, *args)
    r = _run(nc, [arrays], core_ids=[0])
    return r.results[0]["out_0"]
```

```python
from contextlib import ExitStack

import numpy as np

import concourse.bass as bass
from concourse import mybir

F32 = mybir.dt.float32
F32R = mybir.dt.float32r
I32 = mybir.dt.int32
ALU = mybir.AluOpType
ACT = mybir.ActivationFunctionType
AX = mybir.AxisListType

P = 128
D = 2048
TB = 2
TOK = TB * P
NCOL = 512
KD = D // P
EPS = 1e-6
LAMBDA_INIT = 0.2

DA_H, DA_D, DA_V, DA_ROT = 8, 64, 128, 16
RT_H, RT_D, RT_V = 8, 64, 128
MEM_H, MEM_D = 4, 256
DA_THETA, RT_THETA = 500000.0, 10000.0
D_FF = 5632
NF = D_FF // NCOL

DA_Q0, DA_K0, DA_V0 = 0, 1024, 2048
RT_Q0, RT_K0, RT_V0, RT_G0 = 3072, 3584, 4096, 5120
MQ0, GATE0 = 6144, 7168
GATE_DA, GATE_RT, GATE_MEM = GATE0, GATE0 + D, GATE0 + 2 * D

RING = 4
G_KV, G_MQ, G_PROJ, G_MB, G_DB, G_RB, G_OUT, G_F0, G_F = 0, 32, 48, 144, 192, 240, 288, 320, 336
G_END = G_F + 24 * (NF - 1)
U_KV, U_MQ, U_PROJ, U_MB, U_DB, U_RB, U_OUT, U_F0, U_F = 0, 2, 3, 9, 13, 17, 21, 23, 24
U_END = U_F + 3 * (NF - 1)
MEM_PIECES = ((0, 2), (2, 4), (4, 8), (8, 12), (12, 16))
NEG = -1.0e30
FAR = 3.0e7
TWO_PI = (6.28125, 0.0019350051879882812, 3.019916050173085e-07)
ROUND = 12582912.0


def shape_constants():
    da = np.float32(DA_THETA) ** (-np.arange(DA_ROT // 2, dtype=np.float32) * np.float32(2.0) / np.float32(DA_ROT))
    rt = np.float32(RT_THETA) ** (-np.arange(RT_D // 2, dtype=np.float32) * np.float32(2.0) / np.float32(RT_D))
    lg = np.log(np.float32(1.0) - np.float32(2.0) ** (np.float32(-5.0) - np.arange(RT_H, dtype=np.float32)))
    return np.concatenate([da, rt, lg]).astype(np.float32)[None, :]


def program(nc, x, mem, positions, w_in, da_q_norm_g, da_k_norm_g, da_lambda_q1, da_lambda_k1,
            da_lambda_q2, da_lambda_k2, da_subln_g, ret_norm_g, w_mem_kv, mem_q_norm_g,
            mem_k_norm_g, w_o_da, w_o_ret, w_o_mem, w_out, w_ffn_gate, w_ffn_up, w_ffn_down,
            shape_consts, x_t, mem_t, norm_gains, out):
    ds = bass.ds
    NROT = DA_ROT // 2 + RT_D // 2
    R1 = DA_ROT // 2
    with ExitStack() as ctx:
        def sb(name, shape, dt=F32):
            return ctx.enter_context(nc.sbuf_tensor(name, shape, dt))

        def sem(name):
            return ctx.enter_context(nc.semaphore(name))

        raw = sb("raw", [P, RING, 2, NCOL])
        w_hi = sb("w_hi", [P, RING, 2, NCOL], F32R)
        w_lo = sb("w_lo", [P, RING, 2, NCOL], F32R)
        hT_hi = sb("hT_hi", [P, KD, TOK], F32R)
        hT_lo = sb("hT_lo", [P, KD, TOK], F32R)
        oT_hi = sb("oT_hi", [P, KD, TOK], F32R)
        oT_lo = sb("oT_lo", [P, KD, TOK], F32R)
        proj = sb("proj", [P, TB, GATE0])
        kvm = sb("kvm", [P, TB, D])
        sq = sb("sq", [P, TB, 2, 256])
        qn = sb("qn", [P, TB, 2, 256])
        pm = sb("pm", [P, 4, 384])
        ident = sb("ident", [P, P])
        mask = sb("mask", [P, P])
        rel = sb("rel", [P, 256])
        g_cols = sb("g_cols", [P, 3 * KD])
        g_da = sb("g_da", [P, 2, DA_D])
        g_mem = sb("g_mem", [P, 2, MEM_D])
        g_sub = sb("g_sub", [P, DA_V])
        g_ret = sb("g_ret", [P, RT_V])
        lam_s = sb("lam_s", [P, 2])
        lam_e = sb("lam_e", [P, 2])
        neg_lam = sb("neg_lam", [P, 1])
        sc = sb("sc", [P, NROT + RT_H])
        pos_i = sb("pos_i", [P, TB], I32)
        pos_f = sb("pos_f", [P, TB])
        trig = sb("trig", [P, 2, TB, NROT])
        minus_half = sb("minus_half", [P, 16])
        ss = sb("ss", [P, 16])
        ms = sb("ms", [P, 16])
        rstd = sb("rstd", [P, 16])
        row_ss = sb("row_ss", [P, 3, TB])
        x2_ss = sb("x2_ss", [P, TB, 4])
        half_rstd = sb("half_rstd", [P, TB])
        row_ms = sb("row_ms", [P, 3, TB])
        row_rstd = sb("row_rstd", [P, 3, TB])
        mx = sb("mx", [P, 4, 2])
        nmx = sb("nmx", [P, 4, 2])
        den = sb("den", [P, 4, 2])
        rden = sb("rden", [P, 4, 2])
        lrden = sb("lrden", [P, 2, 2])

        sq_flat, qn_flat, pm_flat = (a[:].rearrange(r) for a, r in (
            (sq, "p t k d -> p (t k d)"), (qn, "p t k d -> p (t k d)"), (pm, "p b c -> p (b c)")))
        qkT = sq_flat.rearrange("p (j c) -> p j c", j=2)
        pT = qn_flat[:, 0:768].rearrange("p (j c) -> p j c", j=2)
        osb = pm_flat[:, 0:512].rearrange("p (a c) -> p a c", a=2)
        ret_prod = pm_flat[:, 0:512].rearrange("p (n c) -> p n c", n=4)
        diff_prod = pm_flat[:, 768:1280].rearrange("p (n c) -> p n c", n=4)
        v_head = pm_flat[:, 768:1280].rearrange("p (k d) -> p k d", k=2)
        dec = pm_flat[:, 768:1280].rearrange("p (j c) -> p j c", j=2)
        tanh_g = qn[:, :, :, P:2 * P]
        lam_in = pm_flat[:, 0:256].rearrange("p (a b d) -> p a b d", a=2, b=2)
        lam_pr = pm_flat[:, 256:384].rearrange("p (b d) -> p b d", b=2)
        ang = pm_flat[:, 384:544].rearrange("p (k t n) -> p k t n", k=2, t=TB)
        turns = pm_flat[:, 544:704].rearrange("p (k t n) -> p k t n", k=2, t=TB)
        memT = proj[:, :, 2 * D:3 * D].rearrange("p t (k c) -> p t k c", c=TOK)
        xT = proj[:, :, 0:D].rearrange("p t (k c) -> p t k c", c=TOK)
        gt = proj[:, :, MQ0:MQ0 + NCOL]
        sg = proj[:, :, MQ0 + NCOL:MQ0 + 2 * NCOL]

        acc = [ctx.enter_context(nc.psum_tensor(f"acc{i}", [P, TB, NCOL], F32)) for i in range(2)]
        at = ctx.enter_context(nc.psum_tensor("at", [P, 4, 512], F32))

        loaded = [sem(f"loaded{i}") for i in range(RING)]
        hi_done, lo_done = sem("hi_done"), sem("lo_done")
        pair_used = sem("pair_used")
        acc_free = [sem(f"acc_free{i}") for i in range(2)]
        mem_in, x_in = [sem(f"mem_in{i}") for i in range(TB)], [sem(f"x_in{i}") for i in range(TB)]
        memT_in = [sem(f"memT_in{i}") for i in range(len(MEM_PIECES))]
        xT_in = [sem(f"xT_in{i}") for i in range(4)]
        x_again = sem("x_again")
        const_in = sem("const_in")
        gains_in = sem("gains_in")
        zeroed, masks = sem("zeroed"), sem("masks")
        row_sq, row_sum, row_mean, row_root = sem("row_sq"), sem("row_sum"), sem("row_mean"), sem("row_root")
        row_half = sem("row_half")
        col_ps, col_hi, col_lo = sem("col_ps"), sem("col_hi"), sem("col_lo")
        setup_v, setup_a = sem("setup_v"), sem("setup_a")
        end_done, end_added = sem("end_done"), sem("end_added")
        out_done = sem("out_done")

        def phase_sems(tag, names):
            return {n: sem(f"{tag}_{n}") for n in names}
        M = phase_sems("mem", "squared summed mean root normed values turned copied scored maxed negmax exped recip "
                              "weighed pT_ps pT ov hi lo".split())
        A = phase_sems("da", "squared summed mean root scaled gained rprod rot turned copied scored masked maxed "
                             "negmax exped recip lrecip second mixed pT_ps pT ov osq osum omean oroot onorm oT_ps "
                             "hi lo".split())
        R = phase_sems("ret", "decays tanh rprod rot turned copied scored weighed ov osq osum omean oroot onorm gmul "
                              "gated oT_ps hi lo".split())
        merged = sem("merged")
        ff_ps, ff_hi, ff_lo = sem("ff_ps"), sem("ff_hi"), sem("ff_lo")

        block = ctx.enter_context(nc.Block())

        def tiles(w, row0, col0):
            return w[ds(row0, 2 * P), ds(col0, NCOL)].rearrange("(k p) n -> p k n", p=P)

        w_in2, w_kv2, w_out2 = w_in[0], w_mem_kv[0], w_out[0]
        w_g2, w_u2, w_d2 = w_ffn_gate[0], w_ffn_up[0], w_ffn_down[0]

        @block.sync
        def _(sp):
            def load(w, row0, col0, g, s):
                if not (isinstance(g, int) and g < RING):
                    sp.wait_ge(lo_done, g - RING + 1)
                sp.dma_start(raw[:, s % RING], tiles(w, row0, col0)).then_inc(loaded[s % RING], 16)

            def load_chunk(w, row0, col0, g, s, n=KD // 2):
                for k in range(n):
                    load(w, row0 + 2 * P * k, col0, g + k, s + k)

            def const(dst, src, done):
                sp.dma_start(dst, src).then_inc(done, 16)

            def transposed(dst, src, k0, k1, done):
                sp.dma_start(dst[:, k0 // 8, k0 % 8:(k1 - 1) % 8 + 1, :],
                             src[k0 * P:k1 * P, :].rearrange("(k p) c -> p k c", p=P)).then_inc(done, 16)

            def mem_piece(n):
                transposed(memT, mem_t, *MEM_PIECES[n], memT_in[n])

            def rows(c0, src, t, done):
                sp.dma_start(proj[:, t, c0:c0 + D], src[0, t * P:(t + 1) * P, :]).then_inc(done[t], 16)

            load(w_kv2, 0, 0, 0, 0)
            const(g_cols[:], norm_gains, gains_in)
            mem_piece(0)
            for g in range(1, 32):
                if g in (1, 2, 4, 5):
                    mem_piece((1, 2, 4, 5).index(g) + 1)
                if g in (8, 11):
                    rows(0, mem, (g - 8) // 3, mem_in)
                if g in (15, 19):
                    rows(D, x, (g - 15) // 4, x_in)
                if g in (21, 23, 24, 26):
                    n = (21, 23, 24, 26).index(g)
                    sp.wait_ge(row_sq, 2)
                    transposed(xT, x_t, 4 * n, 4 * n + 4, xT_in[n])
                load(w_kv2, 2 * P * (g % 8), (g // 8) * NCOL, g, g)
            for dst, src in ((g_da[:, 0], da_q_norm_g), (g_da[:, 1], da_k_norm_g), (g_mem[:, 0], mem_q_norm_g),
                             (g_mem[:, 1], mem_k_norm_g), (g_sub[:], da_subln_g), (g_ret[:], ret_norm_g),
                             (lam_in[:, 0, 0], da_lambda_q1), (lam_in[:, 0, 1], da_lambda_q2),
                             (lam_in[:, 1, 0], da_lambda_k1), (lam_in[:, 1, 1], da_lambda_k2), (sc[:], shape_consts)):
                const(dst, src[0].partition_broadcast(P), const_in)
            with nc.allow_non_contiguous_dma(reason="256 positions, once"):
                const(pos_i[:], positions[0].rearrange("(t p) -> p t", p=P), const_in)
            with sp.Fori(0, 2) as n:
                load_chunk(w_in2, 0, n * NCOL + MQ0, n * 8 + G_MQ, 0)
            with sp.Fori(0, 12) as n:
                load_chunk(w_in2, 0, n * NCOL, n * 8 + G_PROJ, 0)
            for gate, wo, g0 in ((GATE_MEM, w_o_mem, G_MB), (GATE_DA, w_o_da, G_DB), (GATE_RT, w_o_ret, G_RB)):
                with sp.Fori(1, 5) as n:
                    load_chunk(w_in2, 0, n * NCOL + (gate - NCOL), n * 12 + (g0 - 12), 0)
                    load_chunk(wo[0], 0, n * NCOL - NCOL, n * 12 + (g0 - 4), 8, 4)
                if gate == GATE_DA:
                    sp.wait_ge(A["lo"], 4)
                    for t in range(TB):
                        sp.dma_start(proj[:, t, 0:D], x[0, t * P:(t + 1) * P, :]).then_inc(x_again, 16)
            with sp.Fori(0, 4) as n:
                load_chunk(w_out2, 0, n * NCOL, n * 8 + G_OUT, 0)
            load_chunk(w_g2, 0, 0, G_F0, 0)
            load_chunk(w_u2, 0, 0, G_F0 + 8, 8)
            with sp.Fori(1, NF) as f:
                g0 = f * 24 + (G_F - 24)
                load_chunk(w_g2, 0, f * NCOL, g0, 0)
                load_chunk(w_u2, 0, f * NCOL, g0 + 8, 8)
                for n in range(4):
                    load_chunk(w_d2, f * NCOL - NCOL, n * NCOL, g0 + (16 + 2 * n), 2 * n, 2)
            for n in range(4):
                load_chunk(w_d2, (NF - 1) * NCOL, n * NCOL, G_END + 2 * n, 2 * n, 2)
            for n in range(3):
                sp.wait_ge(acc_free[n % 2], U_END + n // 2 + 2)
                sp.dma_start(out[0].rearrange("(t p) n -> p t n", p=P)[:, :, n * NCOL:(n + 1) * NCOL],
                             proj[:, :, n * NCOL:(n + 1) * NCOL]).then_inc(out_done, 16)
            for t in range(TB):
                sp.wait_ge(end_added, t + 1)
                sp.dma_start(out[0, t * P:(t + 1) * P, D - NCOL:D], proj[:, t, D - NCOL:D]).then_inc(out_done, 16)
            sp.wait_ge(out_done, 16 * 5)

        @block.gpsimd
        def _(pool):
            nc.gpsimd.memset(ident[:], 0.0).then_inc(zeroed, 1)
            nc.gpsimd.memset(mask[:], 0.0).then_inc(zeroed, 1)
            nc.gpsimd.memset(minus_half[:], -0.5).then_inc(zeroed, 1)
            nc.gpsimd.iota(rel[:], pattern=[[1, 256]], base=0, channel_multiplier=-1,
                           allow_small_or_imprecise_dtypes=True).then_inc(zeroed, 1)
            pool.wait_ge(zeroed, 4)
            nc.gpsimd.affine_select(out=ident[:], in_=ident[:], compare_op=ALU.not_equal, fill=1.0, base=0,
                                    pattern=[[-1, P]], channel_multiplier=1).then_inc(masks, 1)
            nc.gpsimd.affine_select(out=mask[:], in_=mask[:], compare_op=ALU.is_ge, fill=NEG, base=0,
                                    pattern=[[-1, P]], channel_multiplier=1).then_inc(masks, 1)
            nc.gpsimd.affine_select(out=rel[:], in_=rel[:], compare_op=ALU.is_ge, fill=FAR, base=0,
                                    pattern=[[1, 256]], channel_multiplier=-1).then_inc(masks, 1)

            def row_roots(k):
                for t in range(TB):
                    pool.wait_ge(row_mean, 2 * k + t + 1 if k < 2 else 5)
                    nc.gpsimd.tensor_tensor(row_rstd[:, k, t:t + 1], row_ms[:, k, t:t + 1], minus_half[:, 0:1],
                                            ALU.pow).then_inc(row_root, 1)

            def head_roots(ready, done, i, n):
                pool.wait_ge(ready, i + 1)
                nc.gpsimd.tensor_tensor(rstd[:, 0:n], ms[:, 0:n], minus_half[:, 0:n], ALU.pow).then_inc(done, 1)

            row_roots(0)
            row_roots(1)
            with pool.Fori(0, MEM_H) as i:
                head_roots(M["mean"], M["root"], i, 4)
            with pool.Fori(0, 4) as i:
                head_roots(A["mean"], A["root"], i, 16)
                head_roots(A["omean"], A["oroot"], i, 4)
            with pool.Fori(0, 4) as i:
                head_roots(R["omean"], R["oroot"], i, 4)
            row_roots(2)

        @block.scalar
        def _(act):
            def high(g, s):
                act.wait_ge(loaded[s % RING],
                            (g // RING + 2) * 16 if isinstance(g, int) else g * 4 + (32 - 4 * (s % RING)))
                act.wait_ge(pair_used, g + 1)
                act.activation(w_hi[:, s % RING], raw[:, s % RING], ACT.Copy).then_inc(hi_done, 1)

            def row_squares(k, t, ready, c0):
                act.wait_ge(ready, 16)
                if k == 0:
                    act.wait_ge(col_lo, KD)
                else:
                    act.wait_ge(row_sq, t + 1)
                act.activation(proj[:, t, 2 * D:3 * D], proj[:, t, c0:c0 + D], ACT.Square,
                               accum_out=row_ss[:, k, t:t + 1]).then_inc(row_sq, 1)

            def high_input(norm, ks, dst, src):
                for k in ks:
                    act.activation(dst[:, k, :], src[:, k // 8, k % 8, :], ACT.Copy,
                                   scale=g_cols[:, norm * KD + k:norm * KD + k + 1]).then_inc(col_hi, 1)

            def high_columns(n0, ks, dst, scale, shift=0):
                for k in ks:
                    act.wait_ge(col_ps, n0 + k + 1 - 2 * KD)
                    act.activation(dst[:, (k + shift) % KD, :], at[:, k % 4, 0:TOK], ACT.Copy,
                                   scale=scale(k)).then_inc(col_hi, 1)

            def evacuate(g, p, norm, dst):
                act.wait_ge(pair_used, g + 1)
                for t in range(TB):
                    e = act.activation(dst[:, t], acc[p][:, t, :], ACT.Copy, scale=row_rstd[:, norm, t:t + 1])
                e.then_inc(acc_free[p], 1)

            act.wait_ge(zeroed, 4)
            act.activation(nmx[:, 0, 0:1], minus_half[:, 0:1], ACT.Copy)
            for s in range(RING):
                act.wait_ge(loaded[s], 16)
                act.activation(w_hi[:, s], raw[:, s], ACT.Copy).then_inc(hi_done, 1)
                if s == 0:
                    act.wait_ge(gains_in, 16)
                    act.wait_ge(memT_in[0], 16)
                    high_input(0, range(2), oT_hi, memT)
                for n in range(1, 4):
                    if MEM_PIECES[n][0] == 2 + 2 * s:
                        act.wait_ge(memT_in[n], 16)
                high_input(0, range(2 + 2 * s, 4 + 2 * s), oT_hi, memT)

            for s in range(32):
                if s < 3:
                    if s == 1:
                        act.wait_ge(memT_in[4], 16)
                    high_input(0, range(10 + 2 * s, 12 + 2 * s), oT_hi, memT)
                if s in (9, 11):
                    row_squares(0, (s - 9) // 2, mem_in[(s - 9) // 2], 0)
                if s in (17, 19):
                    row_squares(1, (s - 17) // 2, x_in[(s - 17) // 2], D)
                if s in (13, 15, 23, 31):
                    if s == 13:
                        act.wait_ge(row_root, 2)
                    n = (s - 6) // 8 if s == 13 else s // 8
                    evacuate(G_KV + 8 * n + 7, n % 2, 0, kvm[:, :, n * NCOL:(n + 1) * NCOL])
                if 22 <= s < 30:
                    if s % 2 == 0:
                        act.wait_ge(xT_in[(s - 22) // 2], 16)
                    high_input(1, range(2 * s - 44, 2 * s - 42), hT_hi, xT)
                high(G_KV + s, s)

            act.wait_ge(row_root, 4)
            for s in range(16):
                if s == 4:
                    act.wait_ge(setup_v, 11)
                    act.activation(trig[:], ang, ACT.Sin).then_inc(setup_a, 1)
                    act.activation(lam_e[:], lam_s[:], ACT.Exp).then_inc(setup_a, 1)
                if s in (7, 15):
                    c0 = MQ0 + (s // 8) * NCOL
                    evacuate(G_MQ + s, s // 8, 1, proj[:, :, c0:c0 + NCOL])
                high(G_MQ + s, s)

            def projections(i, s, i0):
                if s in (7, 15):
                    evacuate(i * 16 + (G_PROJ + 16 * i0 + s), s // 8, 1,
                             proj[:, :, ds(i * 1024 + (1024 * i0 + (s // 8) * NCOL), NCOL)])
                high(i * 16 + (G_PROJ + 16 * i0 + s), s)

            with act.Fori(0, MEM_H) as i:
                for s in range(16):
                    if s == 0:
                        act.activation(sq[:, :, 0, :], proj[:, :, ds(i * MEM_D + MQ0, MEM_D)], ACT.Square)
                        act.activation(sq[:, :, 1, :], kvm[:, :, ds(i * MEM_D, MEM_D)],
                                       ACT.Square).then_inc(M["squared"], 1)
                    if s == 2:
                        act.activation(v_head, kvm[:, :, ds(i * MEM_D + 1024, MEM_D)],
                                       ACT.Copy).then_inc(M["values"], 1)
                    if s == 4:
                        act.wait_ge(M["turned"], i + 1)
                        act.activation(qkT, at[:, 0:2, :], ACT.Copy).then_inc(M["copied"], 1)
                    if s == 6:
                        act.wait_ge(M["negmax"], i + 1)
                        for t in range(TB):
                            e = act.activation(pm[:, t, 0:256], at[:, 2, t * 256:(t + 1) * 256], ACT.Exp,
                                               bias=nmx[:, 0, t:t + 1], scale=MEM_D ** -0.5,
                                               accum_out=den[:, 0, t:t + 1])
                        e.then_inc(M["exped"], 1)
                    if s == 9:
                        act.wait_ge(M["pT_ps"], i + 1)
                        act.activation(pT[:, :, 0:256], at[:, 3, :].rearrange("p (a b) -> p a b", a=2),
                                       ACT.Copy).then_inc(M["pT"], 1)
                    if s == 11:
                        act.wait_ge(M["ov"], i + 1)
                        act.activation(oT_hi[:, ds(i * 2, 2), :], at[:, 1, :].rearrange("p (a b) -> p a b", a=2),
                                       ACT.Copy).then_inc(M["hi"], 1)
                    projections(i, s, 0)
            def diff_squares(i):
                act.activation(sq[:, :, 0, :], proj[:, :, ds(i * 256 + DA_Q0, 256)], ACT.Square)
                act.activation(sq[:, :, 1, :], proj[:, :, ds(i * 256 + DA_K0, 256)],
                               ACT.Square).then_inc(A["squared"], 1)

            for n in range(32):
                if n == 1:
                    diff_squares(0)
                projections(n // 16, n % 16, 4)

            def gate(i, s, g0, u0):
                if s == 8:
                    act.wait_ge(pair_used, i * 12 + (g0 + 8))
                    act.wait_ge(acc_free[1], i + (u0 + 1))
                    act.wait_ge(row_half, 1)
                    for t in range(TB):
                        e = act.activation(sg[:, t], acc[0][:, t, :], ACT.Tanh, scale=half_rstd[:, t:t + 1])
                    e.then_inc(acc_free[0], 1)

            def diff_attention(i, last):
                for s in range(12):
                    if s == 3:
                        act.wait_ge(A["turned"], i + 1)
                        for j in range(2):
                            e = act.activation(qkT[:, j, :], at[:, 2 * j, :], ACT.Copy)
                        e.then_inc(A["copied"], 1)
                    if s == 5:
                        act.wait_ge(A["negmax"], i + 1)
                        for b in range(4):
                            for t, (c0, c1) in enumerate(((0, 128), (128, 384))):
                                e = act.activation(pm[:, b, c0:c1], at[:, b, c0:c1], ACT.Exp,
                                                   bias=nmx[:, b, t:t + 1], scale=DA_D ** -0.5,
                                                   accum_out=den[:, b, t:t + 1])
                        e.then_inc(A["exped"], 1)
                    if s == 8:
                        act.wait_ge(A["pT_ps"], i + 1)
                        for j in range(2):
                            e = act.activation(pT[:, j, :], at[:, 2 * j, 0:384], ACT.Copy)
                        e.then_inc(A["pT"], 1)
                    gate(i, s, G_MB, U_MB)
                    if s == 9:
                        act.wait_ge(A["ov"], i + 1)
                        for j in range(2):
                            e = act.activation(sq[:, j, 0, :], at[:, 2 * j + 1, 0:256], ACT.Square)
                        e.then_inc(A["osq"], 1)
                    if s == 10 and not last:
                        act.wait_ge(A["osum"], i + 1)
                        diff_squares(i + 1)
                    if s == 11:
                        act.wait_ge(A["oT_ps"], i + 1)
                        act.activation(oT_hi[:, ds(i * 2 + 8, 2), :], at[:, 1, :].rearrange("p (a b) -> p a b", a=2),
                                       ACT.Copy).then_inc(A["hi"], 1)
                    high(i * 12 + (G_MB + s), s)

            with act.Fori(0, 3) as i:
                diff_attention(i, False)
            diff_attention(3, True)

            with act.Fori(0, 4) as i:
                for s in range(12):
                    if s == 0:
                        for j in range(2):
                            e = act.activation(dec[:, j, 0:256], rel[:], ACT.Exp,
                                               scale=sc[:, ds(i * 2 + (NROT + j), 1)])
                        e.then_inc(R["decays"], 1)
                        act.activation(tanh_g, proj[:, :, ds(i * 256 + RT_G0, 256)].rearrange(
                                           "p t (j d) -> p t j d", j=2), ACT.Tanh,
                                       scale=0.5).then_inc(R["tanh"], 1)
                    if s == 3:
                        act.wait_ge(R["turned"], i + 1)
                        act.activation(qkT[:, 0, :], at[:, 0, :], ACT.Copy).then_inc(R["copied"], 1)
                    if s == 7:
                        act.wait_ge(R["ov"], i + 1)
                        act.activation(sq[:, :, 0, :], at[:, 3, :].rearrange("p (a b) -> p a b", a=2),
                                       ACT.Square).then_inc(R["osq"], 1)
                    gate(i, s, G_DB, U_DB)
                    if s == 10:
                        act.wait_ge(R["oT_ps"], i + 1)
                        act.activation(oT_hi[:, ds(i * 2, 2), :], at[:, 0, :].rearrange("p (a b) -> p a b", a=2),
                                       ACT.Copy).then_inc(R["hi"], 1)
                    high(i * 12 + (G_DB + s), s)

            with act.Fori(0, 3) as i:
                for s in range(12):
                    gate(i, s, G_RB, U_RB)
                    high(i * 12 + (G_RB + s), s)
            for s in range(12):
                gate(3, s, G_RB, U_RB)
                if 2 <= s <= 5:
                    high_columns(2 * KD, range(2 * s - 4, 2 * s - 2), oT_hi, lambda k: 0.5, 8)
                high(36 + G_RB + s, s)
            high_columns(2 * KD, range(8, 12), oT_hi, lambda k: 0.5, 8)

            def residual_squares(n):
                act.wait_ge(acc_free[n % 2], U_OUT + n // 2 + 2)
                act.wait_ge(row_sq, 4 + 2 * n)
                for t in range(TB):
                    act.activation(kvm[:, t, 0:NCOL], proj[:, t, n * NCOL:(n + 1) * NCOL], ACT.Square,
                                   accum_out=x2_ss[:, t, n:n + 1]).then_inc(row_sq, 1)

            def residual_columns(n):
                high_columns(3 * KD, range(4 * n, 4 * n + 4), hT_hi, lambda k: g_cols[:, 2 * KD + k:2 * KD + k + 1])

            for s in range(32):
                if s == 2:
                    high_columns(2 * KD, range(12, KD), oT_hi, lambda k: 0.5, 8)
                if s >= 8 and s % 8 == 1:
                    residual_squares(s // 8 - 1)
                if s >= 8 and s % 8 == 2:
                    residual_columns(s // 8 - 1)
                high(G_OUT + s, s)
            residual_squares(3)

            def silu(g, u, f):
                act.wait_ge(pair_used, g + 1)
                if f is not None:
                    act.wait_ge(acc_free[1], u + 1)
                for t in range(TB):
                    e = act.activation(sg[:, t], acc[0][:, t, :], ACT.Silu, scale=row_rstd[:, 2, t:t + 1])
                e.then_inc(acc_free[0], 1)

            def high_acts(f, dst):
                act.wait_ge(ff_ps, f)
                act.activation(dst[:, 0:4, :], at[:, 0:2, :].rearrange("p b (a c) -> p (b a) c", a=2),
                               ACT.Copy).then_inc(ff_hi, 1)

            for s in range(16):
                if s == 2:
                    residual_columns(3)
                if s == 8:
                    act.wait_ge(row_root, 6)
                    silu(G_F0 + 7, U_F0, None)
                high(G_F0 + s, s)
            def feed_forward(f, s):
                if s == 3:
                    high_acts(f, oT_hi)
                if s == 8:
                    silu(f * 24 + (G_F - 24 + 7), f * 3 + (U_F - 3), f)
                high(f * 24 + (G_F - 24 + s), s)

            with act.Fori(1, NF - 1) as f:
                for s in range(24):
                    feed_forward(f, s)
            for s in range(24):
                if s == 19:
                    high_acts(NF, hT_hi)
                feed_forward(NF - 1, s)
            for s in range(4):
                high(G_END + s, s)

        @block.vector
        def _(v):
            def step(ins, s, value):
                ins.then_inc(s, 1)
                v.wait_ge(s, value)

            def low(g, s):
                v.wait_ge(hi_done, g + (RING + 1))
                v.tensor_tensor(w_lo[:, s % RING], raw[:, s % RING], w_hi[:, s % RING].bitcast(F32),
                                ALU.subtract).then_inc(lo_done, 1)

            def row_means(k):
                for t in range(TB):
                    v.wait_ge(row_sq, 2 * k + t + 1)
                    v.tensor_scalar(row_ms[:, k, t:t + 1], row_ss[:, k, t:t + 1], 1.0 / D, EPS, ALU.mult,
                                    ALU.add).then_inc(row_mean, 1)

            def low_columns(n0, ks, dst, hi, scale, shift=0):
                for k in ks:
                    v.wait_ge(col_hi, n0 + k + 1)
                    v.scalar_tensor_tensor(out=dst[:, (k + shift) % KD, :], in0=at[:, k % 4, 0:TOK], scalar=scale(k),
                                           in1=hi[:, (k + shift) % KD, :].bitcast(F32), op0=ALU.mult,
                                           op1=ALU.subtract).then_inc(col_lo, 1)

            def low_input(norm, ks, dst, hi, src):
                for k in ks:
                    v.wait_ge(col_hi, norm * KD + k + 1)
                    v.scalar_tensor_tensor(out=dst[:, k, :], in0=src[:, k // 8, k % 8, :],
                                           scalar=g_cols[:, norm * KD + k:norm * KD + k + 1],
                                           in1=hi[:, k, :].bitcast(F32), op0=ALU.mult,
                                           op1=ALU.subtract).then_inc(col_lo, 1)

            def mean_squares(src, n, width, i, X, summed, mean):
                step(v.tensor_reduce(ss[:, 0:n], src, AX.X, ALU.add), X[summed], i + 1)
                v.tensor_scalar(ms[:, 0:n], ss[:, 0:n], 1.0 / width, EPS, ALU.mult, ALU.add).then_inc(X[mean], 1)

            for p in range(2):
                v.nop().then_inc(acc_free[p], 1)
            for s in range(RING):
                v.wait_ge(hi_done, s + 1)
                v.tensor_tensor(w_lo[:, s], raw[:, s], w_hi[:, s].bitcast(F32), ALU.subtract).then_inc(lo_done, 1)
                low_input(0, range(2 + 2 * s if s else 0, 4 + 2 * s), oT_lo, oT_hi, memT)
            for s in range(32):
                if s < 3:
                    low_input(0, range(10 + 2 * s, 12 + 2 * s), oT_lo, oT_hi, memT)
                if s == 12:
                    row_means(0)
                if s == 20:
                    row_means(1)
                if 22 <= s < 30:
                    low_input(1, range(2 * s - 44, 2 * s - 42), hT_lo, hT_hi, xT)
                low(G_KV + s, s)

            def angles():
                v.wait_ge(const_in, 16 * 12)
                step(v.tensor_copy(pos_f[:], pos_i[:]), setup_v, 1)
                for t in range(TB):
                    for k in range(2):
                        e = v.tensor_scalar(ang[:, k, t, :], sc[:, 0:NROT], pos_f[:, t:t + 1], None, ALU.mult)
                step(e, setup_v, 2)
                for k in range(2):
                    e = v.tensor_scalar(turns[:, k], ang[:, k], 1.0 / (2.0 * np.pi), 0.25 * k, ALU.mult, ALU.add)
                step(e, setup_v, 3)
                step(v.tensor_scalar(turns, turns, ROUND, None, ALU.add), setup_v, 4)
                step(v.tensor_scalar(turns, turns, -ROUND, None, ALU.add), setup_v, 5)
                for n, part in enumerate(TWO_PI):
                    step(v.scalar_tensor_tensor(out=ang, in0=turns, scalar=-part, in1=ang, op0=ALU.mult,
                                                op1=ALU.add), setup_v, 6 + n)
                v.tensor_tensor(lam_pr, lam_in[:, 0], lam_in[:, 1], ALU.mult)
                step(v.tensor_scalar(ang[:, 1], ang[:, 1], 0.5 * np.pi, None, ALU.add), setup_v, 9)
                step(v.tensor_scalar(ang, ang, 3.1415925, -3.1415925, ALU.min, ALU.max), setup_v, 10)
                v.tensor_reduce(lam_s[:], lam_pr[:], AX.X, ALU.add).then_inc(setup_v, 1)

            def rotary_and_lambda():
                v.wait_ge(setup_a, 2)
                step(v.tensor_tensor(neg_lam[:], lam_e[:, 1:2], lam_e[:, 0:1], ALU.subtract), setup_v, 12)
                v.tensor_scalar(neg_lam[:], neg_lam[:], -LAMBDA_INIT, None, ALU.add)
                v.tensor_scalar(g_sub[:], g_sub[:], 1.0 - LAMBDA_INIT, None, ALU.mult)
                step(v.tensor_scalar(g_ret[:], g_ret[:], 0.5, None, ALU.mult), setup_v, 13)
                v.wait_ge(row_root, 4)
                v.tensor_scalar(half_rstd[:], row_rstd[:, 1, :], 0.5, None, ALU.mult).then_inc(row_half, 1)

            for s in range(16):
                if s == 2:
                    angles()
                if s == 6:
                    rotary_and_lambda()
                low(G_MQ + s, s)

            with v.Fori(0, MEM_H) as i:
                for s in range(16):
                    if s == 0:
                        v.wait_ge(M["squared"], i + 1)
                        mean_squares(sq[:].rearrange("p t k d -> p (t k) d"), 4, MEM_D, i, M, "summed", "mean")
                        v.wait_ge(M["root"], i + 1)
                        for t in range(TB):
                            for k, src in enumerate((proj[:, t, ds(i * MEM_D + MQ0, MEM_D)],
                                                     kvm[:, t, ds(i * MEM_D, MEM_D)])):
                                e = v.scalar_tensor_tensor(out=qn[:, t, k, :], in0=src,
                                                           scalar=rstd[:, 2 * t + k:2 * t + k + 1],
                                                           in1=g_mem[:, k, :], op0=ALU.mult, op1=ALU.mult)
                        e.then_inc(M["normed"], 1)
                    if s == 6:
                        v.wait_ge(M["scored"], i + 1)
                        step(v.tensor_reduce(mx[:, 0, :], at[:, 2, :].rearrange("p (t k) -> p t k", t=2), AX.X,
                                             ALU.max), M["maxed"], i + 1)
                        v.tensor_scalar(nmx[:, 0, :], mx[:, 0, :], -MEM_D ** -0.5, None,
                                        ALU.mult).then_inc(M["negmax"], 1)
                    if s == 7:
                        v.wait_ge(M["exped"], i + 1)
                        step(v.reciprocal(rden[:, 0, :], den[:, 0, :]), M["recip"], i + 1)
                        for t in range(TB):
                            e = v.tensor_scalar(pm[:, t, 0:256], pm[:, t, 0:256], rden[:, 0, t:t + 1], None, ALU.mult)
                        e.then_inc(M["weighed"], 1)
                    if s == 11:
                        v.wait_ge(M["hi"], i + 1)
                        v.tensor_tensor(oT_lo[:, ds(i * 2, 2), :], at[:, 1, :].rearrange("p (a b) -> p a b", a=2),
                                        oT_hi[:, ds(i * 2, 2), :].bitcast(F32), ALU.subtract).then_inc(M["lo"], 1)
                    low(i * 16 + (G_PROJ + s), s)
            def diff_means(i):
                v.wait_ge(A["squared"], i + 1)
                mean_squares(sq[:].rearrange("p t k (m d) -> p (t k m) d", d=DA_D), 16, DA_D, i, A,
                             "summed", "mean")

            def diff_normalise(i):
                v.wait_ge(A["root"], i + 1)
                r = rstd[:].rearrange("p (t k m) -> p t k m", t=2, k=2)
                for k, c0 in enumerate((DA_Q0, DA_K0)):
                    e = v.tensor_tensor(qn[:, :, k, :].rearrange("p t (m d) -> p t m d", d=DA_D),
                                        proj[:, :, ds(i * 256 + c0, 256)].rearrange("p t (m d) -> p t m d", d=DA_D),
                                        r[:, :, k, :].unsqueeze(3).to_broadcast([P, 2, 4, DA_D]), ALU.mult)
                step(e, A["scaled"], i + 1)
                for k in range(2):
                    q = qn[:, :, k, :].rearrange("p t (m d) -> p t m d", d=DA_D)
                    e = v.tensor_tensor(q, q, g_da[:, k, :].unsqueeze(1).unsqueeze(1).to_broadcast([P, 2, 4, DA_D]),
                                        ALU.mult)
                step(e, A["gained"], i + 1)

            def diff_rotate(i):
                q = qn[:].rearrange("p t k (m d) -> p t (k m) d", d=DA_D)
                sin = trig[:, 0, :, 0:R1].unsqueeze(2).to_broadcast([P, 2, 8, R1])
                cos = trig[:, 1, :, 0:R1].unsqueeze(2).to_broadcast([P, 2, 8, R1])
                tv = diff_prod.rearrange("p n (t m d) -> p n t m d", t=2, m=8)
                x1, x2 = q[:, :, :, 0:R1], q[:, :, :, R1:2 * R1]
                v.tensor_tensor(tv[:, 0], x1, cos, ALU.mult)
                v.tensor_tensor(tv[:, 1], x2, sin, ALU.mult)
                v.tensor_tensor(tv[:, 2], x2, cos, ALU.mult)
                step(v.tensor_tensor(tv[:, 3], x1, sin, ALU.mult), A["rprod"], i + 1)
                v.tensor_tensor(x1, tv[:, 0], tv[:, 1], ALU.subtract)
                v.tensor_tensor(x2, tv[:, 2], tv[:, 3], ALU.add).then_inc(A["rot"], 1)

            for n in range(32):
                if n == 2:
                    diff_means(0)
                if n == 4:
                    diff_normalise(0)
                if n == 5:
                    diff_rotate(0)
                low(G_PROJ + 64 + n, n)

            def gated(i, s, g0, u0, first, n0):
                if s == 11:
                    v.wait_ge(pair_used, i * 12 + (g0 + 12))
                    v.wait_ge(acc_free[0], i + (u0 + 2))
                    dst = kvm[:, :, ds(i * NCOL, NCOL)]
                    e = v.scalar_tensor_tensor(out=dst if first else gt, in0=sg, scalar=1.0, in1=acc[1][:],
                                               op0=ALU.add, op1=ALU.mult)
                    e.then_inc(acc_free[1], 1)
                    if not first:
                        v.wait_ge(acc_free[1], i + (u0 + 2))
                        v.tensor_tensor(dst, dst, gt, ALU.add).then_inc(merged, 1)
                        v.wait_ge(merged, i + (n0 + 1))

            def diff_attention(i, last):
                for s in range(12):
                    if s == 4:
                        v.wait_ge(A["scored"], i + 1)
                        sd = at[:].rearrange("p b (h c) -> p b h c", h=2)[:, :, :, 0:P]
                        step(v.tensor_tensor(sd, sd, mask[:].unsqueeze(1).unsqueeze(1).to_broadcast([P, 4, 2, P]),
                                             ALU.add), A["masked"], i + 1)
                        v.tensor_reduce(mx[:, :, 0:1], at[:, :, 0:128], AX.X, ALU.max)
                        step(v.tensor_reduce(mx[:, :, 1:2], at[:, :, 128:384], AX.X, ALU.max), A["maxed"], i + 1)
                        v.tensor_scalar(nmx[:], mx[:], -DA_D ** -0.5, None, ALU.mult).then_inc(A["negmax"], 1)
                    if s == 5:
                        v.wait_ge(A["exped"], i + 1)
                        step(v.reciprocal(rden[:], den[:]), A["recip"], i + 1)
                        step(v.tensor_scalar(lrden[:], rden[:].rearrange("p (j m) t -> p j m t", m=2)[:, :, 1, :],
                                             neg_lam[:, 0:1], None, ALU.mult), A["lrecip"], i + 1)
                        spans = ((0, 128), (128, 384))
                        for j in range(2):
                            for t, (c0, c1) in enumerate(spans):
                                e = v.tensor_scalar(pm[:, 2 * j + 1, c0:c1], pm[:, 2 * j + 1, c0:c1],
                                                    lrden[:, j, t:t + 1], None, ALU.mult)
                        step(e, A["second"], i + 1)
                        for j in range(2):
                            for t, (c0, c1) in enumerate(spans):
                                e = v.scalar_tensor_tensor(out=pm[:, 2 * j, c0:c1], in0=pm[:, 2 * j, c0:c1],
                                                           scalar=rden[:, 2 * j, t:t + 1], in1=pm[:, 2 * j + 1, c0:c1],
                                                           op0=ALU.mult, op1=ALU.add)
                        e.then_inc(A["mixed"], 1)
                    if s == 9:
                        v.wait_ge(A["osq"], i + 1)
                        mean_squares(sq[:, :, 0, :].rearrange("p j (t d) -> p j t d", t=2), 4, DA_V, i, A,
                                     "osum", "omean")
                        v.wait_ge(A["oroot"], i + 1)
                        for j in range(2):
                            for t in range(TB):
                                n = 2 * j + t
                                e = v.scalar_tensor_tensor(out=osb[:, j, t * P:(t + 1) * P],
                                                           in0=at[:, 2 * j + 1, t * P:(t + 1) * P],
                                                           scalar=rstd[:, n:n + 1], in1=g_sub[:], op0=ALU.mult,
                                                           op1=ALU.mult)
                        e.then_inc(A["onorm"], 1)
                    if s == 10 and not last:
                        diff_means(i + 1)
                    if s == 11 and not last:
                        diff_normalise(i + 1)
                        diff_rotate(i + 1)
                    if s == 11:
                        v.wait_ge(A["hi"], i + 1)
                        v.tensor_tensor(oT_lo[:, ds(i * 2 + 8, 2), :], at[:, 1, :].rearrange("p (a b) -> p a b", a=2),
                                        oT_hi[:, ds(i * 2 + 8, 2), :].bitcast(F32), ALU.subtract).then_inc(A["lo"], 1)
                    gated(i, s, G_MB, U_MB, True, 0)
                    low(i * 12 + (G_MB + s), s)

            with v.Fori(0, 3) as i:
                diff_attention(i, False)
            diff_attention(3, True)

            with v.Fori(0, 4) as i:
                for s in range(12):
                    if s == 0:
                        H = RT_D // 2
                        for t in range(TB):
                            qk = proj[:, t, RT_Q0:RT_V0].rearrange("p (k c) -> p k c", k=2)[:, :, ds(i * 128, 128)]
                            qk = qk.rearrange("p k (j d) -> p k j d", j=2)
                            x1, x2 = qk[:, :, :, 0:H], qk[:, :, :, H:2 * H]
                            sin = trig[:, 0, t, R1:NROT].unsqueeze(1).unsqueeze(1).to_broadcast([P, 2, 2, H])
                            cos = trig[:, 1, t, R1:NROT].unsqueeze(1).unsqueeze(1).to_broadcast([P, 2, 2, H])
                            tv = ret_prod.rearrange("p n (k j d) -> p n k j d", k=2, j=2)
                            dst = qn[:, t, :, 0:128].rearrange("p k (j d) -> p k j d", j=2)
                            v.tensor_tensor(tv[:, 0], x1, cos, ALU.mult)
                            v.tensor_tensor(tv[:, 1], x2, sin, ALU.mult)
                            v.tensor_tensor(tv[:, 2], x2, cos, ALU.mult)
                            step(v.tensor_tensor(tv[:, 3], x1, sin, ALU.mult), R["rprod"], i * 2 + (t + 1))
                            v.tensor_tensor(dst[:, :, :, 0:H], tv[:, 0], tv[:, 1], ALU.subtract)
                            step(v.tensor_tensor(dst[:, :, :, H:2 * H], tv[:, 2], tv[:, 3], ALU.add), R["rot"],
                                 i * 2 + (t + 1))
                    if s == 5:
                        v.wait_ge(R["scored"], i + 1)
                        v.wait_ge(R["decays"], i + 1)
                        for j in range(2):
                            for c0, c1 in ((0, 256), (256, 384)):
                                e = v.scalar_tensor_tensor(out=pm[:, j, c0:c1], in0=at[:, 1 + j, c0:c1],
                                                           scalar=RT_D ** -0.5, in1=dec[:, j, 0:c1 - c0],
                                                           op0=ALU.mult, op1=ALU.mult)
                        e.then_inc(R["weighed"], 1)
                    if s == 7:
                        v.wait_ge(R["tanh"], i + 1)
                        for t in range(TB):
                            e = v.scalar_tensor_tensor(out=tanh_g[:, t], in0=tanh_g[:, t], scalar=1.0,
                                               in1=proj[:, t, ds(i * 256 + RT_G0, 256)].rearrange(
                                                   "p (j d) -> p j d", j=2), op0=ALU.add,
                                               op1=ALU.mult)
                        e.then_inc(R["gmul"], 1)
                        v.wait_ge(R["osq"], i + 1)
                        mean_squares(sq[:, :, 0, :].rearrange("p t (j d) -> p t j d", j=2), 4, RT_V, i, R,
                                     "osum", "omean")
                        v.wait_ge(R["oroot"], i + 1)
                        for n in range(4):
                            e = v.scalar_tensor_tensor(out=osb[:, n // 2, (n % 2) * P:(n % 2 + 1) * P],
                                                       in0=at[:, 3, n * P:(n + 1) * P], scalar=rstd[:, n:n + 1],
                                                       in1=g_ret[:], op0=ALU.mult, op1=ALU.mult)
                        step(e, R["onorm"], i + 1)
                        v.wait_ge(R["gmul"], i + 1)
                        o4 = osb.rearrange("p t (j d) -> p t j d", j=2)
                        v.tensor_tensor(o4, o4, tanh_g, ALU.mult).then_inc(R["gated"], 1)
                    if s == 10:
                        v.wait_ge(R["hi"], i + 1)
                        v.tensor_tensor(oT_lo[:, ds(i * 2, 2), :], at[:, 0, :].rearrange("p (a b) -> p a b", a=2),
                                        oT_hi[:, ds(i * 2, 2), :].bitcast(F32), ALU.subtract).then_inc(R["lo"], 1)
                    gated(i, s, G_DB, U_DB, False, 0)
                    low(i * 12 + (G_DB + s), s)

            with v.Fori(0, 3) as i:
                for s in range(12):
                    gated(i, s, G_RB, U_RB, False, 4)
                    low(i * 12 + (G_RB + s), s)
            for s in range(12):
                gated(3, s, G_RB, U_RB, False, 4)
                if 2 <= s <= 5:
                    low_columns(2 * KD, range(2 * s - 4, 2 * s - 2), oT_lo, oT_hi, lambda k: 0.5, 8)
                low(36 + G_RB + s, s)
            low_columns(2 * KD, range(8, 12), oT_lo, oT_hi, lambda k: 0.5, 8)

            def residual(g, p, dst):
                v.wait_ge(pair_used, g + 1)
                v.tensor_tensor(dst, acc[p][:], dst, ALU.add).then_inc(acc_free[p], 1)

            v.wait_ge(x_again, 32)
            def residual_columns(n):
                low_columns(3 * KD, range(4 * n, 4 * n + 4), hT_lo, hT_hi,
                            lambda k: g_cols[:, 2 * KD + k:2 * KD + k + 1])

            for s in range(32):
                if s == 2:
                    low_columns(2 * KD, range(12, KD), oT_lo, oT_hi, lambda k: 0.5, 8)
                if s >= 8 and s % 8 == 2:
                    residual_columns(s // 8 - 1)
                if s % 8 == 7:
                    n = s // 8
                    residual(G_OUT + s, n % 2, proj[:, :, n * NCOL:(n + 1) * NCOL])
                low(G_OUT + s, s)

            def activations(g, u, f):
                v.wait_ge(pair_used, g + 1)
                v.wait_ge(acc_free[0], u + 2)
                if f is not None:
                    v.wait_ge(ff_ps, f)
                for t in range(TB):
                    e = v.scalar_tensor_tensor(out=gt[:, t], in0=acc[1][:, t, :], scalar=row_rstd[:, 2, t:t + 1],
                                               in1=sg[:, t], op0=ALU.mult, op1=ALU.mult)
                e.then_inc(acc_free[1], 1)

            def low_acts(f, dst, hi):
                v.wait_ge(ff_hi, f)
                v.tensor_tensor(dst[:, 0:4, :], at[:, 0:2, :].rearrange("p b (a c) -> p (b a) c", a=2),
                                hi[:, 0:4, :].bitcast(F32), ALU.subtract).then_inc(ff_lo, 1)

            for s in range(16):
                if s == 2:
                    residual_columns(3)
                if s == 3:
                    v.wait_ge(row_sq, 4 + 8)
                    step(v.tensor_reduce(row_ss[:, 2, :], x2_ss[:], AX.X, ALU.add), row_sum, 1)
                    v.tensor_scalar(row_ms[:, 2, :], row_ss[:, 2, :], 1.0 / D, EPS, ALU.mult,
                                    ALU.add).then_inc(row_mean, 1)
                if s == 15:
                    v.wait_ge(row_root, 6)
                    activations(G_F0 + s, U_F0, None)
                low(G_F0 + s, s)
            def feed_forward(f, s):
                if s == 3:
                    low_acts(f, oT_lo, oT_hi)
                if s == 15:
                    activations(f * 24 + (G_F - 24 + s), f * 3 + (U_F - 3), f)
                if s in (17, 19, 21, 23):
                    n = (s - 17) // 2
                    residual(f * 24 + (G_F - 24 + s), n % 2, proj[:, :, n * NCOL:(n + 1) * NCOL])
                low(f * 24 + (G_F - 24 + s), s)

            with v.Fori(1, NF - 1) as f:
                for s in range(24):
                    feed_forward(f, s)
            for s in range(24):
                if s == 19:
                    low_acts(NF, hT_lo, hT_hi)
                feed_forward(NF - 1, s)
            for s in range(8):
                if s == 7:
                    for t in range(TB):
                        v.wait_ge(end_done, t + 1)
                        v.tensor_tensor(proj[:, t, D - NCOL:D], acc[1][:, t, :], proj[:, t, D - NCOL:D],
                                        ALU.add).then_inc(end_added, 1)
                elif s % 2 == 1:
                    n = s // 2
                    residual(G_END + s, n % 2, proj[:, :, n * NCOL:(n + 1) * NCOL])
                if s < 4:
                    low(G_END + s, s)

        @block.tensor
        def _(pe):
            def three_passes(s, hi, lo, k0, p, k, t, first, last):
                tok = slice(t * P, (t + 1) * P)
                for n, (a, w) in enumerate(((hi, w_hi), (hi, w_lo), (lo, w_hi))):
                    e = pe.matmul(acc[p][:, t, :], a[:, k0 + k, tok], w[:, s % RING, k, :],
                                  start=first and k == 0 and n == 0, stop=last and k == 1 and n == 2)
                return e

            def pair(g, s, hi, lo, k0, p, first, last, col=None):
                pe.wait_ge(lo_done, g + 1)
                if col is not None:
                    pe.wait_ge(col_lo, col)
                for k in range(2):
                    for t in range(TB):
                        e = three_passes(s, hi, lo, k0, p, k, t, first, last)
                return e

            def chunk_pair(g, s, hi, lo, k0, kk, nk, u, p, col=None):
                if kk == 0:
                    pe.wait_ge(acc_free[p], u + 1)
                e = pair(g, s, hi, lo, k0 + 2 * kk, p, kk == 0, kk == nk - 1, col)
                e.then_inc(pair_used, 1)

            def turn(out, src):
                return pe.transpose(out, src, ident[:])

            def turn_columns(n0, ks, src, c0):
                for k in ks:
                    pe.wait_ge(col_lo, n0 + k - 3)
                    for t in range(TB):
                        e = turn(at[:, k % 4, t * P:(t + 1) * P], src[:, t, c0 + k * P:c0 + (k + 1) * P])
                    e.then_inc(col_ps, 1)

            pe.wait_ge(masks, 1)
            for n in range(24):
                turn(at[:, 3, 0:P], ident[:])
            for s in range(32):
                chunk_pair(G_KV + s, s, oT_hi, oT_lo, 0, s % 8, 8, U_KV + s // 16, (s // 8) % 2,
                           2 * s + 2 if s < 8 else None)
            pe.wait_ge(col_lo, 2 * KD)
            for s in range(16):
                chunk_pair(G_MQ + s, s, hT_hi, hT_lo, 0, s % 8, 8, U_MQ, s // 8)

            with pe.Fori(0, MEM_H) as i:
                for s in range(16):
                    chunk_pair(i * 16 + (G_PROJ + s), s, hT_hi, hT_lo, 0, s % 8, 8, i + U_PROJ, s // 8)
                    if s == 3:
                        pe.wait_ge(M["normed"], i + 1)
                        for k in range(2):
                            for h in range(2):
                                for t in range(TB):
                                    e = turn(at[:, k, h * 256 + t * P:h * 256 + (t + 1) * P],
                                             qn[:, t, k, h * P:(h + 1) * P])
                        e.then_inc(M["turned"], 1)
                    if s == 5:
                        pe.wait_ge(M["copied"], i + 1)
                        for t in range(TB):
                            for h in range(2):
                                e = pe.matmul(at[:, 2, t * 256:(t + 1) * 256],
                                              qkT[:, 0, h * 256 + t * P:h * 256 + (t + 1) * P],
                                              qkT[:, 1, h * 256:(h + 1) * 256], start=h == 0, stop=h == 1)
                        e.then_inc(M["scored"], 1)
                    if s == 8:
                        pe.wait_ge(M["weighed"], i + 1)
                        for k in range(2):
                            for t in range(TB):
                                e = turn(at[:, 3, k * 256 + t * P:k * 256 + (t + 1) * P], pm[:, t, k * P:(k + 1) * P])
                        e.then_inc(M["pT_ps"], 1)
                    if s == 10:
                        pe.wait_ge(M["values"], i + 1)
                        pe.wait_ge(M["pT"], i + 1)
                        for h in range(2):
                            for k in range(2):
                                e = pe.matmul(at[:, 1, h * 256:(h + 1) * 256],
                                              v_head[:, k, h * P:(h + 1) * P], pT[:, k, 0:256],
                                              start=k == 0, stop=k == 1)
                        e.then_inc(M["ov"], 1)
            with pe.Fori(0, 2) as i:
                for s in range(16):
                    chunk_pair(i * 16 + (G_PROJ + 64 + s), s, hT_hi, hT_lo, 0, s % 8, 8, i + (U_PROJ + 4), s // 8)

            def gate_branch(i, s, g0, u0, k0, outputs, count):
                if s == 8:
                    pe.wait_ge(outputs, count)
                if s < 8:
                    chunk_pair(i * 12 + (g0 + s), s, hT_hi, hT_lo, 0, s, 8, i + u0, 0)
                else:
                    chunk_pair(i * 12 + (g0 + s), s, oT_hi, oT_lo, k0, s - 8, 4, i + u0, 1)

            with pe.Fori(0, 4) as i:
                for s in range(12):
                    gate_branch(i, s, G_MB, U_MB, 0, M["lo"], MEM_H)
                    if s == 2:
                        pe.wait_ge(A["rot"], i + 1)
                        for j in range(2):
                            for k in range(2):
                                for t in range(TB):
                                    e = turn(at[:, 2 * j, k * 256 + t * P:k * 256 + (t + 1) * P],
                                             qn[:, t, k, j * P:(j + 1) * P])
                        e.then_inc(A["turned"], 1)
                    if s == 3:
                        pe.wait_ge(A["copied"], i + 1)
                        for j in range(2):
                            for m in range(2):
                                row = slice(m * DA_D, (m + 1) * DA_D)
                                pe.matmul(at[:, 2 * j + m, 0:128], qkT[row, j, 0:128], qkT[row, j, 256:384],
                                          start=True, stop=True)
                                e = pe.matmul(at[:, 2 * j + m, 128:384], qkT[row, j, 128:256],
                                              qkT[row, j, 256:512], start=True, stop=True)
                        e.then_inc(A["scored"], 1)
                    if s == 7:
                        pe.wait_ge(A["mixed"], i + 1)
                        for j in range(2):
                            for n in range(3):
                                e = turn(at[:, 2 * j, n * P:(n + 1) * P], pm[:, 2 * j, n * P:(n + 1) * P])
                        e.then_inc(A["pT_ps"], 1)
                    if s == 8:
                        pe.wait_ge(A["pT"], i + 1)
                        for j in range(2):
                            v0 = proj[:, 0, ds(i * 256 + (DA_V0 + j * P), P)]
                            v1 = proj[:, 1, ds(i * 256 + (DA_V0 + j * P), P)]
                            pe.matmul(at[:, 2 * j + 1, 0:128], pT[:, j, 0:128], v0, start=True, stop=True)
                            pe.matmul(at[:, 2 * j + 1, 128:256], pT[:, j, 128:256], v0, start=True, stop=False)
                            e = pe.matmul(at[:, 2 * j + 1, 128:256], pT[:, j, 256:384], v1, start=False, stop=True)
                        e.then_inc(A["ov"], 1)
                    if s == 11:
                        pe.wait_ge(A["onorm"], i + 1)
                        for j in range(2):
                            for t in range(TB):
                                e = turn(at[:, 1, j * 256 + t * P:j * 256 + (t + 1) * P], osb[:, j, t * P:(t + 1) * P])
                        e.then_inc(A["oT_ps"], 1)

            with pe.Fori(0, 4) as i:
                for s in range(12):
                    gate_branch(i, s, G_DB, U_DB, 8, A["lo"], 4)
                    if s == 2:
                        pe.wait_ge(R["rot"], i * 2 + 2)
                        for k in range(2):
                            for t in range(TB):
                                e = turn(at[:, 0, k * 256 + t * P:k * 256 + (t + 1) * P], qn[:, t, k, 0:128])
                        e.then_inc(R["turned"], 1)
                    if s == 4:
                        pe.wait_ge(R["copied"], i + 1)
                        for j in range(2):
                            row = slice(j * RT_D, (j + 1) * RT_D)
                            pe.matmul(at[:, 1 + j, 0:256], qkT[row, 0, 256:384], qkT[row, 0, 0:256],
                                      start=True, stop=True)
                            e = pe.matmul(at[:, 1 + j, 256:384], qkT[row, 0, 384:512], qkT[row, 0, 128:256],
                                          start=True, stop=True)
                        e.then_inc(R["scored"], 1)
                    if s == 6:
                        pe.wait_ge(R["weighed"], i + 1)
                        for j in range(2):
                            v0 = proj[:, 0, ds(i * 256 + (RT_V0 + j * P), P)]
                            v1 = proj[:, 1, ds(i * 256 + (RT_V0 + j * P), P)]
                            o0, o1 = at[:, 3, j * P:(j + 1) * P], at[:, 3, 256 + j * P:256 + (j + 1) * P]
                            pe.matmul(o0, pm[:, j, 0:128], v0, start=True, stop=True)
                            pe.matmul(o1, pm[:, j, 128:256], v0, start=True, stop=False)
                            e = pe.matmul(o1, pm[:, j, 256:384], v1, start=False, stop=True)
                        e.then_inc(R["ov"], 1)
                    if s == 9:
                        pe.wait_ge(R["gated"], i + 1)
                        for j in range(2):
                            for t in range(TB):
                                e = turn(at[:, 0, j * 256 + t * P:j * 256 + (t + 1) * P], osb[:, t, j * P:(j + 1) * P])
                        e.then_inc(R["oT_ps"], 1)

            with pe.Fori(0, 3) as i:
                for s in range(12):
                    gate_branch(i, s, G_RB, U_RB, 0, R["lo"], 4)
            for s in range(12):
                gate_branch(3, s, G_RB, U_RB, 0, R["lo"], 4)
                if s == 1:
                    pe.wait_ge(merged, 7)
                if 1 <= s <= 4:
                    turn_columns(2 * KD, range(2 * s - 2, 2 * s), kvm, 0)
            turn_columns(2 * KD, range(8, 12), kvm, 0)
            for s in range(32):
                chunk_pair(G_OUT + s, s, oT_hi, oT_lo, 8 - 16 * (s % 8 > 3), s % 8, 8, U_OUT + s // 16, (s // 8) % 2,
                           2 * KD + 2 * s + 2 if s < 8 else None)
                if s == 1:
                    pe.wait_ge(merged, 8)
                    turn_columns(2 * KD, range(12, KD), kvm, 0)
                if s >= 8 and s % 8 == 0:
                    n = s // 8 - 1
                    pe.wait_ge(acc_free[n % 2], U_OUT + n // 2 + 2)
                    turn_columns(3 * KD, range(4 * n, 4 * n + 4), proj, 0)

            def turn_acts(drained):
                pe.wait_ge(acc_free[1], drained)
                for k in range(4):
                    for t in range(TB):
                        c0 = (k % 2) * 256 + t * P
                        e = turn(at[:, k // 2, c0:c0 + P], gt[:, t, k * P:(k + 1) * P])
                e.then_inc(ff_ps, 1)

            for s in range(16):
                chunk_pair(G_F0 + s, s, hT_hi, hT_lo, 0, s % 8, 8, U_F0, s // 8, 3 * KD + 2 * s + 2 if s < 8 else None)
                if s == 1:
                    pe.wait_ge(acc_free[1], U_F0 + 1)
                    turn_columns(3 * KD, range(12, KD), proj, 0)
            def feed_forward(f, s):
                g, u = f * 24 + (G_F - 24 + s), f * 3 + (U_F - 3)
                if s < 16:
                    chunk_pair(g, s, hT_hi, hT_lo, 0, s % 8, 8, u, s // 8)
                else:
                    if s == 16:
                        pe.wait_ge(ff_lo, f)
                    n = (s - 16) // 2
                    chunk_pair(g, s, oT_hi, oT_lo, 0, s % 2, 2, u + (1 + n // 2), n % 2)
                if s == 2:
                    turn_acts(f * 3 + (U_F - 2))

            with pe.Fori(1, NF - 1) as f:
                for s in range(24):
                    feed_forward(f, s)
            for s in range(24):
                feed_forward(NF - 1, s)
                if s == 17:
                    turn_acts(U_END - 1)
            pe.wait_ge(ff_lo, NF)
            for s in range(7):
                chunk_pair(G_END + s, s, hT_hi, hT_lo, 0, s % 2, 2, U_END + s // 4, (s // 2) % 2)
            pe.wait_ge(lo_done, G_END + 8)
            for t in range(TB):
                for k in range(2):
                    e = three_passes(7, hT_hi, hT_lo, 2, 1, k, t, False, True)
                e.then_inc(end_done, 1)


_INS = ['x', 'mem', 'positions', 'w_in', 'da_q_norm_g', 'da_k_norm_g', 'da_lambda_q1', 'da_lambda_k1',
        'da_lambda_q2', 'da_lambda_k2', 'da_subln_g', 'ret_norm_g', 'w_mem_kv', 'mem_q_norm_g',
        'mem_k_norm_g', 'w_o_da', 'w_o_ret', 'w_o_mem', 'w_out', 'w_ffn_gate', 'w_ffn_up', 'w_ffn_down']


def kernel(**inputs):
    import concourse.bacc as _bacc
    from concourse.bass_utils import run_bass_kernel_spmd as _run

    nc = _bacc.Bacc("TRN2", target_bir_lowering=False, num_devices=1)
    arrays, args = {}, []
    laid_out = {
        "shape_consts": shape_constants(),
        "x_t": inputs["x"][0].T, "mem_t": inputs["mem"][0].T,
        "norm_gains": np.concatenate([inputs[n].reshape(KD, P).T for n in ("mem_norm_g", "attn_norm_g", "ffn_norm_g")],
                                     axis=1),
    }
    for name in _INS + list(laid_out):
        a = np.ascontiguousarray(laid_out[name] if name in laid_out else inputs[name])
        arrays[f"in_{name}"] = a
        args.append(nc.dram_tensor(f"in_{name}", a.shape, mybir.dt.from_np(a.dtype), kind="ExternalInput").ap())
    args.append(nc.dram_tensor("out_0", (1, TOK, D), F32, kind="ExternalOutput").ap())
    program(nc, *args)
    r = _run(nc, [arrays], core_ids=[0])
    return r.results[0]["out_0"]
```
